# Optimizing a Trainium2 kernel written in Bass

```python
import math
import jax, jax.numpy as jnp
from jax import lax
import numpy as np

D_MODEL = 2048
BATCH = 1
SEQ = 256
DEPTH = 1

BW = D_MODEL // 4
N_BRANCH = 3
HG_HEADS = 4
HG_DIM = BW // HG_HEADS
HG_CHUNK = 16
S5_GROUP = 16
S5_GROUPS = BW // S5_GROUP
S5_STATE = 64
DT_MIN = 0.001
DT_MAX = 0.1
SB_HEADS = 4
SB_DIM = BW // SB_HEADS
SB_BLOCK = 128
D_FF = 256 * ((8 * D_MODEL // 3 + 255) // 256)
CONV_W = 3
EPS = 1e-6
IN_COLS = 8 * BW + N_BRANCH * D_MODEL

kernel_name = "hybrid_hgrn2_s5_stickbreak_block"

def rms_norm(x, g):
    xf = x.astype(jnp.float32)
    y = xf * lax.rsqrt(jnp.mean(xf * xf, axis=-1, keepdims=True) + EPS)
    return (y * g.astype(jnp.float32)).astype(x.dtype)

def hgrn2_mixer(q, f_logit, i_in, g, lb, norm_g):
    f32 = jnp.float32
    B_, L_, _ = q.shape
    nc = L_ // HG_CHUNK
    lb = lb.astype(f32)
    logf = jnp.logaddexp(jnp.log(lb), jnp.log1p(-lb) + jax.nn.log_sigmoid(f_logit.astype(f32)))
    k = -jnp.expm1(logf)

    def to_chunks(t):
        return t.astype(f32).reshape(B_, nc, HG_CHUNK, HG_HEADS, HG_DIM).transpose(1, 0, 3, 2, 4)

    qc, kc, vc, lfc = to_chunks(q), to_chunks(k), to_chunks(i_in), to_chunks(logf)
    causal = jnp.tril(jnp.ones((HG_CHUNK, HG_CHUNK), dtype=bool))

    def step(S, inp):
        qb, kb, vb, lfb = inp
        b = jnp.cumsum(lfb, axis=2)
        diff = b[:, :, :, None, :] - b[:, :, None, :, :]
        decay = jnp.exp(jnp.where(causal[:, :, None], diff, -jnp.inf))
        scores = jnp.einsum('bhtd,bhsd,bhtsd->bhts', qb, kb, decay)
        o = scores @ vb + jnp.einsum('bhtd,bhde->bhte', qb * jnp.exp(b), S)
        b_last = b[:, :, -1:, :]
        S_new = jnp.exp(b_last[:, :, 0, :, None]) * S + jnp.einsum(
            'bhsd,bhse->bhde', kb * jnp.exp(b_last - b), vb)
        return S_new, o

    S0 = jnp.zeros((B_, HG_HEADS, HG_DIM, HG_DIM), f32)
    _, o = lax.scan(step, S0, (qc, kc, vc, lfc))
    o = o.transpose(1, 0, 3, 2, 4).reshape(B_, L_, HG_HEADS, HG_DIM)
    o = o * lax.rsqrt(jnp.mean(o * o, axis=-1, keepdims=True) + EPS)
    o = o.reshape(B_, L_, BW) * norm_g.astype(f32) * jax.nn.silu(g.astype(f32))
    return o.astype(q.dtype)

def s5_mixer(u, a_re, a_im, b_re, b_im, c_re, c_im, d_skip, log_dt, w_glu):
    f32 = jnp.float32
    B_, L_, _ = u.shape
    uf = u.astype(f32)
    ug = uf.reshape(B_, L_, S5_GROUPS, S5_GROUP)
    dt = jnp.exp(log_dt.astype(f32))[:, None]
    lr, li = a_re.astype(f32), a_im.astype(f32)
    mag = jnp.exp(lr * dt)
    ab_re, ab_im = mag * jnp.cos(li * dt), mag * jnp.sin(li * dt)
    den = lr * lr + li * li
    nr, ni = ab_re - 1.0, ab_im
    z_re = (nr * lr + ni * li) / den
    z_im = (ni * lr - nr * li) / den
    br, bi = b_re.astype(f32), b_im.astype(f32)
    bb_re = z_re[..., None] * br - z_im[..., None] * bi
    bb_im = z_re[..., None] * bi + z_im[..., None] * br
    bu_re = jnp.einsum('gnc,blgc->blgn', bb_re, ug)
    bu_im = jnp.einsum('gnc,blgc->blgn', bb_im, ug)
    a_sc_re = jnp.broadcast_to(ab_re, bu_re.shape)
    a_sc_im = jnp.broadcast_to(ab_im, bu_im.shape)

    def combine(e1, e2):
        a1r, a1i, b1r, b1i = e1
        a2r, a2i, b2r, b2i = e2
        return (a2r * a1r - a2i * a1i, a2r * a1i + a2i * a1r,
                a2r * b1r - a2i * b1i + b2r, a2r * b1i + a2i * b1r + b2i)

    _, _, xs_re, xs_im = lax.associative_scan(combine, (a_sc_re, a_sc_im, bu_re, bu_im), axis=1)
    y = (jnp.einsum('gcn,blgn->blgc', c_re.astype(f32), xs_re)
         - jnp.einsum('gcn,blgn->blgc', c_im.astype(f32), xs_im))
    y = y.reshape(B_, L_, BW) + d_skip.astype(f32) * uf
    a = jax.nn.gelu(y)
    hg = a @ w_glu.astype(f32)
    out = hg[..., :BW] * jax.nn.sigmoid(hg[..., BW:])
    return out.astype(u.dtype)

def stick_breaking_mixer(q, k, v, q_g, k_g):
    f32 = jnp.float32
    B_, L_, _ = q.shape

    def heads(t):
        return t.astype(f32).reshape(B_, L_, SB_HEADS, SB_DIM).transpose(0, 2, 1, 3)

    qh = rms_norm(heads(q), q_g)
    kh = rms_norm(heads(k), k_g)
    vh = heads(v)
    nb = L_ // SB_BLOCK
    scale = SB_DIM ** -0.5
    outs = []
    for i in range(nb):
        n = i + 1
        qb = qh[:, :, i * SB_BLOCK:(i + 1) * SB_BLOCK]
        kb = kh[:, :, :n * SB_BLOCK].reshape(B_, SB_HEADS, n, SB_BLOCK, SB_DIM)
        vb = vh[:, :, :n * SB_BLOCK].reshape(B_, SB_HEADS, n, SB_BLOCK, SB_DIM)
        q_pos = i * SB_BLOCK + jnp.arange(SB_BLOCK)
        k_pos = jnp.arange(n * SB_BLOCK).reshape(n, SB_BLOCK)
        mask = k_pos[None] < q_pos[:, None, None]
        z = jnp.einsum('bhqd,bhnkd->bhqnk', qb, kb) * scale
        log_keep = jnp.where(mask, jax.nn.log_sigmoid(-z), 0.0)
        within = lax.cumsum(log_keep, axis=4, reverse=True) - log_keep
        blk_tot = jnp.sum(log_keep, axis=4)
        later = lax.cumsum(blk_tot, axis=3, reverse=True) - blk_tot
        w = jnp.where(mask, jnp.exp(jax.nn.log_sigmoid(z) + within + later[..., None]), 0.0)
        outs.append(jnp.einsum('bhqnk,bhnkd->bhqd', w, vb))
    o = jnp.concatenate(outs, axis=2)
    o = o.transpose(0, 2, 1, 3).reshape(B_, L_, BW)
    return o.astype(q.dtype)

def causal_depthwise_conv(u, w):
    return lax.conv_general_dilated(
        u, w[:, None, :].astype(u.dtype), window_strides=(1,), padding=[(CONV_W - 1, 0)],
        dimension_numbers=('NWC', 'WIO', 'NWC'), feature_group_count=u.shape[-1])

def setup_inputs(seed: int = 0) -> dict:
    key = jax.random.key(seed)
    ks = jax.random.split(key, 24)
    f32 = jnp.float32
    nrm = lambda k, shape, s: jax.random.normal(k, shape, f32) * s
    gain = lambda k, shape: 1.0 + 0.02 * jax.random.normal(k, shape, f32)
    return {
        "x": nrm(ks[0], (BATCH, SEQ, D_MODEL), 1.0),
        "w_in": nrm(ks[1], (DEPTH, D_MODEL, IN_COLS), D_MODEL ** -0.5),
        "norm_mix_g": gain(ks[2], (DEPTH, D_MODEL)),
        "hg_lb_logits": nrm(ks[3], (DEPTH, BW), 0.1),
        "hg_norm_g": gain(ks[4], (DEPTH, BW)),
        "s5_a_re": -0.5 + nrm(ks[5], (DEPTH, S5_GROUPS, S5_STATE), 0.01),
        "s5_a_im": math.pi * jnp.arange(S5_STATE, dtype=f32) + nrm(ks[6], (DEPTH, S5_GROUPS, S5_STATE), 0.01),
        "s5_b_re": nrm(ks[7], (DEPTH, S5_GROUPS, S5_STATE, S5_GROUP), (2 * S5_GROUP) ** -0.5),
        "s5_b_im": nrm(ks[8], (DEPTH, S5_GROUPS, S5_STATE, S5_GROUP), (2 * S5_GROUP) ** -0.5),
        "s5_c_re": nrm(ks[9], (DEPTH, S5_GROUPS, S5_GROUP, S5_STATE), (2 * S5_STATE) ** -0.5),
        "s5_c_im": nrm(ks[10], (DEPTH, S5_GROUPS, S5_GROUP, S5_STATE), (2 * S5_STATE) ** -0.5),
        "s5_d": nrm(ks[11], (DEPTH, BW), 1.0),
        "s5_log_dt": jax.random.uniform(ks[12], (DEPTH, S5_GROUPS), f32, math.log(DT_MIN), math.log(DT_MAX)),
        "s5_w_glu": nrm(ks[13], (DEPTH, BW, 2 * BW), BW ** -0.5),
        "sb_q_g": gain(ks[14], (DEPTH, SB_DIM)),
        "sb_k_g": gain(ks[15], (DEPTH, SB_DIM)),
        "w_branch": nrm(ks[16], (DEPTH, N_BRANCH, BW, D_MODEL), BW ** -0.5),
        "w_out": nrm(ks[17], (DEPTH, D_MODEL, D_MODEL), D_MODEL ** -0.5),
        "norm_ffn_g": gain(ks[18], (DEPTH, D_MODEL)),
        "w_up": nrm(ks[19], (DEPTH, D_MODEL, 2 * D_FF), D_MODEL ** -0.5),
        "conv_w": nrm(ks[20], (DEPTH, CONV_W, 2 * D_FF), CONV_W ** -0.5),
        "w_down": nrm(ks[21], (DEPTH, D_FF, D_MODEL), D_FF ** -0.5),
    }

def reference(x, w_in, norm_mix_g, hg_lb_logits, hg_norm_g, s5_a_re, s5_a_im, s5_b_re, s5_b_im,
              s5_c_re, s5_c_im, s5_d, s5_log_dt, s5_w_glu, sb_q_g, sb_k_g, w_branch, w_out,
              norm_ffn_g, w_up, conv_w, w_down):
    lb_all = jnp.cumsum(jax.nn.softmax(hg_lb_logits.astype(jnp.float32), axis=0), axis=0)
    lb_all = lb_all - lb_all[0:1]
    split_at = [BW * i for i in range(1, 9)]
    for l in range(DEPTH):
        h = rms_norm(x, norm_mix_g[l])
        proj = h @ w_in[l]
        hq, hf, hi, hg, su, sq, sk, sv, gates = jnp.split(proj, split_at, axis=-1)
        o_a = hgrn2_mixer(hq, hf, hi, hg, lb_all[l], hg_norm_g[l])
        o_b = s5_mixer(su, s5_a_re[l], s5_a_im[l], s5_b_re[l], s5_b_im[l], s5_c_re[l], s5_c_im[l],
                       s5_d[l], s5_log_dt[l], s5_w_glu[l])
        o_c = stick_breaking_mixer(sq, sk, sv, sb_q_g[l], sb_k_g[l])
        gate = jax.nn.sigmoid(gates)
        merged = (gate[..., :D_MODEL] * (o_a @ w_branch[l, 0])
                  + gate[..., D_MODEL:2 * D_MODEL] * (o_b @ w_branch[l, 1])
                  + gate[..., 2 * D_MODEL:] * (o_c @ w_branch[l, 2]))
        x = x + merged @ w_out[l]
        hf2 = rms_norm(x, norm_ffn_g[l])
        up = causal_depthwise_conv(hf2 @ w_up[l], conv_w[l])
        x = x + (jax.nn.silu(up[..., :D_FF]) * up[..., D_FF:]) @ w_down[l]
    return x


_drawn_inputs = setup_inputs


def setup_inputs(seed=0):
    import zlib

    import numpy as np

    out = dict(_drawn_inputs(seed))
    spreads = {}
    factors = {'norm_mix_g': 3.145,
     'hg_norm_g': 8.0,
     's5_a_re': 64.0,
     's5_a_im': 45.656,
     's5_b_re': 64.0,
     's5_b_im': 63.28,
     's5_c_re': 63.4,
     's5_c_im': 64.0,
     's5_log_dt': 46.64,
     'sb_q_g': 24.622,
     'sb_k_g': 26.676,
     'norm_ffn_g': 11.202}
    for name, (base, spread) in spreads.items():
        noise = np.random.default_rng([zlib.crc32(name.encode()), seed]).standard_normal(out[name].shape)
        drawn = base * np.exp(spread * noise) if base else spread * noise
        out[name] = __import__('jax').numpy.asarray(drawn.astype(out[name].dtype))
    for name, factor in factors.items():
        out[name] = (out[name] * factor).astype(out[name].dtype)
    return out
```

```python
from contextlib import ExitStack

import concourse.bass as bass
from concourse import mybir

F32 = mybir.dt.float32
F32R = mybir.dt.float32r
I32 = mybir.dt.int32
U8 = mybir.dt.uint8
ALU = mybir.AluOpType
ACT = mybir.ActivationFunctionType

P = 128
D_MODEL = 2048
SEQ = 256
BW = D_MODEL // 4
HEADS = BW // P
D_FF = 256 * ((8 * D_MODEL // 3 + 255) // 256)
KT = D_MODEL // P
FT = D_FF // P
CT = BW // P
N_BRANCH = 3
S5_GROUPS, S5_STATE, S5_CH = 32, 64, 16
ST = S5_GROUPS * S5_STATE // P
EPS = 1e-6
LEVELS = 8

HG_F, HG_Q, HG_I, HG_G, S5_U, SB_Q, SB_K, SB_V = range(8)

RING = 4
PIECE = 8
BANKS = 4
DOWN_PIECES = [PIECE] * (FT // PIECE) + [FT % PIECE]

IN_TILES = 8 * CT + N_BRANCH * KT
GLU_TILES = 2 * CT
BR_TILES = N_BRANCH * KT
OUT_TILES = KT
UP_TILES = 2 * FT
DOWN_TILES = KT
GLU_T = IN_TILES
BR_T = GLU_T + GLU_TILES
OUT_T = BR_T + BR_TILES
UP_T = OUT_T + OUT_TILES
DOWN_T = UP_T + UP_TILES
GLU_P = 2 * IN_TILES
BR_P = GLU_P + GLU_TILES // 2
OUT_P = BR_P + 2 * KT
UP_P = OUT_P + 2 * OUT_TILES
DOWN_P = UP_P + 2 * UP_TILES
assert all(x % RING == 0 for x in (GLU_P, BR_P, OUT_P, UP_P, DOWN_P, GLU_T, BR_T, OUT_T, UP_T, DOWN_T))

PRODUCTS = (["norm1", "s5_bT"] + ["lev0", "lev1", "hg_vT"] + [f"lev{k}" for k in range(2, LEVELS + 1)]
            + ["hg_o", "hg_ss", "q_ss", "k_ss", "sb_vT", "z0", "z1", "within0", "within1", "sb_o"]
            + ["bu0", "bu1", "bu2", "s5_y0", "bu3", "bu4", "s5_y1", "bu5", "bu6", "s5_y2", "bu7", "s5_y3", "norm2"])
M = {name: m for m, name in enumerate(PRODUCTS)}

AT = {"norm1": 3, "s5_bT": 6, "hg_vT": 14, "hg_o": 29, "hg_ss": 30, "q_ss": 34, "k_ss": 34, "sb_vT": 35,
      "z0": 38, "z1": 38, "within0": 40, "within1": 40, "sb_o": 42}
AT.update({f"lev{k}": 11 + 2 * k for k in range(LEVELS + 1)})
AT.update({f"bu{k}": 43 + 3 * k for k in range(8)})
AT.update({f"s5_y{c}": 50 + 6 * c for c in range(4)})

MAGIC = 12582912.0
TWO_PI = 6.283185307179586
TWO_PI_HI = 6.28125
BELOW_PI = 3.1415925


def layer(nc, xT, w_in, w_glu, w_br, w_out, w_up, w_down, norm_mix, norm_ffn, hg_gain, s5_small, s5_b, s5_c,
          s5_skip, sb_gain, conv, out):
    ctx = ExitStack()
    with ctx:
        def sb(name, shape, dt=F32, scope=None):
            return (scope or ctx).enter_context(nc.sbuf_tensor(name, shape, dt))

        raw = [sb(f"raw{s}", [P, PIECE * P]) for s in range(RING)]
        w_hi = [sb(f"w_hi{s}", [P, PIECE * P], F32R) for s in range(RING)]
        w_lo = [sb(f"w_lo{s}", [P, PIECE * P], F32R) for s in range(RING)]
        half = [sb(f"half{s}", [P, SEQ]) for s in range(2)]
        ones = sb("ones", [P, P])
        eye = sb("eye", [P, P])
        upper = sb("upper", [P, P])
        lower = sb("lower", [P, P])
        level_mask = sb("level_mask", [P, LEVELS, P], U8)
        gain_mix = sb("gain_mix", [P, KT])
        gain_ffn = sb("gain_ffn", [P, KT])
        gain_hg = sb("gain_hg", [P, HEADS])
        gain_sb = sb("gain_sb", [P, 2])
        skip_s5 = sb("skip_s5", [P, CT])
        half_pi = sb("half_pi", [P, 1])
        taps = sb("taps", [P, UP_TILES, 3])
        rstd = sb("rstd", [P, SEQ])
        var = sb("var", [P, SEQ])
        root = sb("root", [P, SEQ])

        late = ExitStack()
        act = sb("act", [P, FT, 2, SEQ], F32R, late)
        x1 = sb("x1", [P, KT, SEQ], F32, late)
        h2 = sb("h2", [P, KT, 2, SEQ], F32R, late)
        sum_u = sb("sum_u", [P, 2, SEQ], F32, late)
        padded = sb("padded", [P, 2, SEQ + 2], F32, late)
        convd = sb("convd", [P, 4, SEQ], F32, late)
        silu = sb("silu", [P, SEQ], F32, late)
        late.close()

        early = ExitStack()
        a_in = sb("a_in", [P, KT, 2, SEQ], F32R, early)
        gates = sb("gates", [P, N_BRANCH * KT, SEQ], F32, early)
        s5_in = sb("s5_in", [P, 3, ST], F32, early)
        s5_t = sb("s5_t", [P, 12, ST], F32, early)
        s5_bT = sb("s5_bT", [P, 2, CT, P], F32, early)
        s5_cT = sb("s5_cT", [P, 2, ST, 2, S5_CH], F32, early)
        time_f = sb("time_f", [P, SEQ], F32, early)
        proj0 = sb("proj0", [P, 5, CT, SEQ], F32, early)
        mixing = ExitStack()
        proj1 = sb("proj1", [P, 3, CT, SEQ], F32, mixing)
        tmp = sb("tmp", [P, 7, 1024], F32, mixing)
        mixing.close()
        splits = ExitStack()
        glu_in = sb("glu_in", [P, CT, 2, SEQ], F32R, splits)
        o_sb = sb("o_sb", [P, CT, 2, SEQ], F32R, splits)
        o_hg = sb("o_hg", [P, CT, 2, SEQ], F32R, splits)
        o_s5 = sb("o_s5", [P, CT, 2, SEQ], F32R, splits)
        gated = sb("gated", [P, 4, SEQ], F32, splits)
        merged = sb("merged", [P, 2, SEQ], F32, splits)
        splits.close()
        early.close()
        x_first = gates[:, 0:KT, :]
        squares = gates[:, KT:2 * KT, :]

        def group(g):
            return proj0[:, g, :, :] if g < 5 else proj1[:, g - 5, :, :]

        def proj(n):
            return group(n // CT)[:, n % CT, :] if n < 8 * CT else gates[:, n - 8 * CT, :]

        def flat(x):
            return x.rearrange("p a b -> p (a b)")

        T = [tmp[:, i, :] for i in range(7)]
        T4 = [t.rearrange("p (c t) -> p c t", c=4) for t in T]
        T2 = [tmp[:, i, :].rearrange("p (s t) -> p s t", t=P) for i in range(7)]

        bank = [ctx.enter_context(nc.psum_tensor(f"bank{b}", [P, 512], F32)) for b in range(BANKS)]
        pair = [ctx.enter_context(nc.psum_tensor(f"pair{b}", [P, 1024], F32)) for b in range(2)]

        def product(name):
            return pair[M[name] % 2]

        sems = {}

        def S(name):
            if name not in sems:
                sems[name] = ctx.enter_context(nc.semaphore(name))
            return sems[name]

        raw_landed = [S(f"raw_landed{s}") for s in range(RING)]
        hi_ready, lo_ready, piece_used = S("hi_ready"), S("lo_ready"), S("piece_used")
        half_copied, tile_summed, tile_scaled = S("half_copied"), S("tile_summed"), S("tile_scaled")
        product_done = S("product_done")
        pair_taken = [S("pair_taken0"), S("pair_taken1")]

        counts = {}

        def link(eng, ins, name):
            counts[name] = counts.get(name, 0) + 1
            ins.then_inc(S(name), 1)
            eng.wait_ge(S(name), counts[name])

        def wait_product(eng, name):
            eng.wait_ge(product_done, M[name] + 1)

        def taken(ins, name):
            return ins.then_inc(pair_taken[M[name] % 2], 1)

        def wait_taken(eng, name):
            eng.wait_ge(pair_taken[M[name] % 2], M[name] // 2 + 1)

        block = ctx.enter_context(nc.Block())

        @block.sync
        def _(sp):
            def load(p, c, src, width=PIECE * P):
                if not (isinstance(p, int) and p < RING):
                    sp.wait_ge(lo_ready, p - (RING - 1))
                sp.dma_start(raw[c % RING][:, 0:width], src).then_inc(raw_landed[c % RING], 16)

            for q in range(4):
                sp.dma_start(x_first[:, 4 * q:4 * q + 4, :], xT[:, 4 * q:4 * q + 4, :]).then_inc(S(f"x_landed{q}"), 16)
                load(q, q, w_in[q])
            with sp.Fori(1, GLU_P // RING) as i:
                for c in range(RING):
                    load(i * RING + c, c, w_in[i * RING + c])
            for c in range(CT):
                load(GLU_P + c, c, w_glu[c])
            with sp.Fori(0, KT // 2) as i:
                for c in range(RING):
                    blocks = PIECE if c % 2 == 0 else N_BRANCH * CT - PIECE
                    load(i * RING + (BR_P + c), c, w_br[i * 2 + c // 2, :, (c % 2) * PIECE * P:(c % 2 * PIECE + blocks) * P],
                         blocks * P)
            with sp.Fori(0, 2 * OUT_TILES // RING) as i:
                for c in range(RING):
                    load(i * RING + (OUT_P + c), c, w_out[i * RING + c])
            with sp.Fori(0, 2 * UP_TILES // RING) as i:
                for c in range(RING):
                    load(i * RING + (UP_P + c), c, w_up[i * RING + c])
            with sp.Fori(0, DOWN_TILES // 2) as i:
                c = 0
                for t in range(2):
                    at = 0
                    for blocks in DOWN_PIECES:
                        load(i * (2 * len(DOWN_PIECES)) + (DOWN_P + c), c, w_down[i * 2 + t, :, at * P:(at + blocks) * P], blocks * P)
                        at += blocks
                        c += 1

        @block.tensor
        def _(pe):
            def piece(b, p, c, blocks, rhs, first, last):
                if p is not None:
                    pe.wait_ge(lo_ready, p + 1)
                w, l = w_hi[c % RING], w_lo[c % RING]
                for n, k in enumerate(blocks):
                    a = rhs(n)
                    pe.matmul(bank[b][:, :], w[:, k * P:(k + 1) * P], a.rearrange("p a t -> p (a t)"),
                              start=first and n == 0, stop=False, skip_group_check=True)
                    mm = pe.matmul(bank[b][:, 0:SEQ], l[:, k * P:(k + 1) * P], a[:, 0, :],
                                   start=False, stop=last and n == len(blocks) - 1, skip_group_check=True)
                return mm

            def bank_free(n):
                if not (isinstance(n, int) and n < BANKS):
                    pe.wait_ge(tile_summed, n - (BANKS - 1))

            def start_product(name):
                m = M[name]
                if m >= 2:
                    pe.wait_ge(pair_taken[m % 2], m // 2)
                return product(name)

            def fp32_product(name, ops):
                out_ = start_product(name)
                for (p0, p1, c0, c1), lhsT, rhs, start, stop in ops:
                    mm = pe.matmul(out_[p0:p1, c0:c1], lhsT, rhs, start=start, stop=stop, skip_group_check=True)
                mm.then_inc(product_done, 1)

            def transposes(name, blocks):
                out_ = start_product(name)
                for i, b in enumerate(blocks):
                    mm = pe.transpose(out_[:, i * P:(i + 1) * P], b, eye[:, :])
                mm.then_inc(product_done, 1)

            def level(k):
                if k == 0:
                    pe.wait_ge(S("hg_k"), 1)
                    pe.wait_ge(tile_scaled, CT * (HG_Q + 1))
                    ops = [((0, P, (4 * b + h) * P, (4 * b + h + 1) * P), T4[2][:, h, b * P:(b + 1) * P],
                            group(HG_Q)[:, h, b * P:(b + 1) * P], True, True) for b in range(2) for h in range(HEADS)]
                else:
                    pe.wait_ge(S("hg_factors"), 2 * k)
                    W = T4[4 + k % 2]
                    if k < LEVELS:
                        ops = [((0, P, (4 * b + h) * P, (4 * b + h + 1) * P), W[:, h, b * P:(b + 1) * P],
                                W[:, h, b * P:(b + 1) * P], True, True) for b in range(2) for h in range(HEADS)]
                    else:
                        ops = [((0, P, h * P, (h + 1) * P), W[:, h, 0:P], W[:, h, P:SEQ], True, True) for h in range(HEADS)]
                fp32_product(f"lev{k}", ops)

            def mixers(n):
                if n == AT["norm1"]:
                    pe.wait_ge(S("x_sq_sum"), 4)
                    fp32_product("norm1", [((0, P, 0, SEQ), ones[:, :], squares[:, 0, :], True, True)])
                if n == AT["s5_bT"]:
                    pe.wait_ge(S("s5_bb"), 4)
                    transposes("s5_bT", [T[1][:, (4 * r + c) * P:(4 * r + c + 1) * P] for r in range(2) for c in range(CT)])
                for k in range(LEVELS + 1):
                    if n == AT[f"lev{k}"]:
                        level(k)
                if n == AT["hg_vT"]:
                    pe.wait_ge(tile_scaled, CT * (HG_I + 1))
                    transposes("hg_vT", [group(HG_I)[:, h, b * P:(b + 1) * P] for b in range(2) for h in range(HEADS)])
                if n == AT["hg_o"]:
                    for name in ("hg_vT", "lev7", "lev8"):
                        wait_taken(pe, name)
                    v = group(HG_F).rearrange("p c (b t) -> p (c b) t", b=2)
                    ops = []
                    for h in range(HEADS):
                        ops += [((0, P, h * SEQ, h * SEQ + P), v[:, h, :], T2[6][:, h, :], True, True),
                                ((0, P, h * SEQ + P, (h + 1) * SEQ), v[:, h, :], T2[0][:, h, :], True, False),
                                ((0, P, h * SEQ + P, (h + 1) * SEQ), v[:, 4 + h, :], T2[6][:, 4 + h, :], False, True)]
                    fp32_product("hg_o", ops)
                for name, sem, src in (("hg_ss", None, T[1]), ("q_ss", "q_sq", T[0]), ("k_ss", "k_sq", T[1])):
                    if n == AT[name]:
                        if sem:
                            pe.wait_ge(S(sem), 1)
                        else:
                            wait_taken(pe, "hg_o")
                        fp32_product(name, [((0, P, c * 512, (c + 1) * 512), ones[:, :], src[:, c * 512:(c + 1) * 512], True, True)
                                            for c in range(2)])
                if n == AT["sb_vT"]:
                    pe.wait_ge(tile_scaled, CT * (SB_V + 1))
                    transposes("sb_vT", [group(SB_V)[:, h, b * P:(b + 1) * P] for b in range(2) for h in range(HEADS)])
                for hh in range(2):
                    if n == AT[f"z{hh}"]:
                        pe.wait_ge(S("q_normed"), 1)
                        pe.wait_ge(S("k_normed"), 1)
                        q, k = group(SB_Q), group(SB_K)
                        fp32_product(f"z{hh}", [((0, P, i * SEQ, (i + 1) * SEQ), k[:, 2 * hh + i, 0:P], q[:, 2 * hh + i, :], True, True)
                                                for i in range(2)]
                                     + [((0, P, 512 + i * P, 512 + (i + 1) * P), k[:, 2 * hh + i, P:SEQ], q[:, 2 * hh + i, P:SEQ], True, True)
                                        for i in range(2)])
                    if n == AT[f"within{hh}"]:
                        pe.wait_ge(S("sb_masked"), 2 * (hh + 1))
                        sp_ = tmp[:, 4:6, :].rearrange("p a b -> p (a b)")[:, 768 * hh:768 * (hh + 1)]
                        ops = []
                        for i in range(2):
                            ops += [((0, P, i * SEQ, (i + 1) * SEQ), lower[:, :], sp_[:, i * SEQ:(i + 1) * SEQ], True, False),
                                    ((0, P, i * SEQ + P, (i + 1) * SEQ), ones[:, :], sp_[:, 512 + i * P:512 + (i + 1) * P], False, True)]
                        for i in range(2):
                            ops += [((0, P, 512 + i * P, 512 + (i + 1) * P), lower[:, :], sp_[:, 512 + i * P:512 + (i + 1) * P], True, True)]
                        fp32_product(f"within{hh}", ops)
                if n == AT["sb_o"]:
                    pe.wait_ge(S("sb_w"), 4)
                    wait_taken(pe, "sb_vT")
                    v = group(HG_Q).rearrange("p c (b t) -> p (c b) t", b=2)
                    w = tmp[:, 0:2, :].rearrange("p a b -> p (a b)")
                    ops = []
                    for h in range(HEADS):
                        at = 768 * (h // 2)
                        i = h % 2
                        ops += [((0, P, h * SEQ, (h + 1) * SEQ), v[:, h, :], w[:, at + i * SEQ:at + (i + 1) * SEQ], True, False),
                                ((0, P, h * SEQ + P, (h + 1) * SEQ), v[:, 4 + h, :], w[:, at + 512 + i * P:at + 512 + (i + 1) * P], False, True)]
                    fp32_product("sb_o", ops)
                for k in range(8):
                    if n == AT[f"bu{k}"]:
                        if k == 0:
                            wait_taken(pe, "s5_bT")
                            pe.wait_ge(tile_scaled, CT * (S5_U + 1))
                        ops = []
                        for i in range(2):
                            for r in range(2):
                                s = 2 * k + i
                                rows = slice(32 * (s % 4), 32 * (s % 4) + 32)
                                ops.append(((0, P, (2 * i + r) * SEQ, (2 * i + r + 1) * SEQ), s5_bT[rows, r, s // 4, :],
                                            group(S5_U)[rows, s // 4, :], True, True))
                        fp32_product(f"bu{k}", ops)
                for c in range(CT):
                    if n == AT[f"s5_y{c}"]:
                        pe.wait_ge(S("s5_x"), 4 * (c + 1))
                        ops = []
                        for i in range(4):
                            ops += [((32 * i, 32 * i + 32, 0, SEQ), s5_cT[:, r, 4 * c + i, :, :].rearrange("p a b -> p (a b)"),
                                     proj1[:, r, i, :], r == 0, r == 1) for r in range(2)]
                        fp32_product(f"s5_y{c}", ops)

            def a_in_block(n, k):
                if n == 0:
                    pe.wait_ge(S("a_in_lo"), k + 1)
                return a_in[:, k, :, :]

            for n in range(IN_TILES):
                bank_free(n)
                for h in range(2):
                    mm = piece(n % BANKS, 2 * n + h, 2 * n + h, range(PIECE), lambda k: a_in_block(n, PIECE * h + k), h == 0, h == 1)
                    mm.then_inc(piece_used, 1)
                mixers(n)

            pe.wait_ge(S("glu_in_lo"), 1)
            for m in range(CT):
                for i in range(2):
                    n = GLU_T + 2 * m + i
                    bank_free(n)
                    mm = piece(n % BANKS, GLU_P + m if i == 0 else None, GLU_P + m, range(CT * i, CT * (i + 1)),
                               lambda k: glu_in[:, k, :, :], True, True)
                    mm.then_inc(piece_used if i else S("glu_first"), 1)

            pe.wait_ge(S("o_split"), 2)

            def branch_tile(i, j):
                t = 3 * j
                for b, (c, lo, src) in enumerate(((0, 0, o_hg), (0, CT, o_sb), (1, 0, o_s5))):
                    n = i * (3 * RING) + (BR_T + t + b)
                    bank_free(n)
                    if b == 2:
                        pe.wait_ge(S("o_split"), 3)
                    mm = piece((t + b) % BANKS, i * (2 * RING) + (BR_P + 2 * j + c) if b != 1 else None, 2 * j + c,
                               range(lo, lo + CT), lambda k: src[:, k, :, :], True, True)
                    mm.then_inc(S("br_first") if b == 0 else piece_used, 1)

            with pe.Fori(0, KT // RING) as i:
                for j in range(RING):
                    branch_tile(i, j)

            pe.wait_ge(S("merged_lo"), KT)
            with pe.Fori(0, OUT_TILES // BANKS) as i:
                for j in range(BANKS):
                    bank_free(i * BANKS + (OUT_T + j))
                    for h in range(2):
                        mm = piece(j, i * (2 * BANKS) + (OUT_P + 2 * j + h), 2 * j + h, range(PIECE),
                                   lambda k: a_in[:, PIECE * h + k, :, :], h == 0, h == 1)
                        mm.then_inc(piece_used, 1)

            def up_body(i):
                for j in range(BANKS):
                    bank_free(i * BANKS + (UP_T + j))
                    for h in range(2):
                        mm = piece(j, i * (2 * BANKS) + (UP_P + 2 * j + h), 2 * j + h, range(PIECE),
                                   lambda k: h2[:, PIECE * h + k, :, :], h == 0, h == 1)
                        mm.then_inc(piece_used, 1)
                    if isinstance(i, int) and j == 0:
                        pe.wait_ge(S("x1_sq_sum"), KT)
                        fp32_product("norm2", [((0, P, 0, SEQ), ones[:, :], root[:, :], True, True)])

            pe.wait_ge(S("h2_lo"), KT)
            up_body(0)
            with pe.Fori(1, UP_TILES // BANKS) as i:
                up_body(i)

            pe.wait_ge(S("act_lo"), FT)
            with pe.Fori(0, DOWN_TILES // BANKS) as i:
                c = 0
                for j in range(BANKS):
                    bank_free(i * BANKS + (DOWN_T + j))
                    at = 0
                    for blocks in DOWN_PIECES:
                        mm = piece(j, i * (BANKS * len(DOWN_PIECES)) + (DOWN_P + c), c, range(blocks),
                                   lambda k: act[:, at + k, :, :], at == 0, at + blocks == FT)
                        mm.then_inc(piece_used, 1)
                        at += blocks
                        c += 1

        HG_FF, HG_QQ, HG_II, HG_GG, UU, SQ, SK = (group(g) for g in (HG_F, HG_Q, HG_I, HG_G, S5_U, SB_Q, SB_K))
        Z = tmp[:, 0:2, :].rearrange("p a b -> p (a b)")[:, 0:1536]
        LOG1P = tmp[:, 2:4, :].rearrange("p a b -> p (a b)")[:, 0:1536]
        SOFTP = tmp[:, 4:6, :].rearrange("p a b -> p (a b)")[:, 0:1536]

        def halves(x, h):
            v = x.rearrange("p c (n r t) -> p (c n) r t", r=2, t=h)
            return v[:, :, 0, :], v[:, :, 1, :]

        def bc(x, shape):
            return x.broadcast_to(shape)

        def s5_tables(g):
            return (T4[2], T4[3]) if g % 2 == 0 else (T4[0], T4[1])

        def s5_slice(k):
            return slice(2 * (k % 2), 2 * (k % 2) + 2)

        SIDX = {n: i for i, n in enumerate(("dt", "mag", "theta", "turns", "r", "cos", "sin", "t1", "t2", "t3", "zr", "zi"))}

        def s5v(name):
            return s5_t[:, SIDX[name], :]

        @block.scalar
        def _(act_e):
            def hi(i, per, p0, blocks=PIECE):
                p, s = i * per + p0, p0 % RING
                act_e.wait_ge(raw_landed[s], i * (16 * per // RING) + 16 * (p0 // RING + 1))
                if not (isinstance(p, int) and p < RING):
                    act_e.wait_ge(piece_used, p - (RING - 1))
                act_e.activation(w_hi[s][:, 0:blocks * P], raw[s][:, 0:blocks * P], ACT.Copy).then_inc(hi_ready, 1)

            def copy_half(n, j, done, value):
                act_e.wait_ge(done, value)
                if not (isinstance(n, int) and n < 2):
                    act_e.wait_ge(tile_summed, n - 1)
                act_e.activation(half[j % 2][:, :], bank[j % BANKS][:, SEQ:2 * SEQ], ACT.Copy).then_inc(half_copied, 1)

            def run(name, out_, in_, func, **kw):
                link(act_e, act_e.activation(out_, in_, func, **kw), name)

            def sigmoid_gates(b):
                act_e.wait_ge(tile_scaled, 8 * CT + 4 * (b + 1))
                g = flat(gates[:, 4 * b:4 * b + 4, :])
                act_e.activation(g, g, ACT.Sigmoid).then_inc(S("gate_ready"), 1)

            def mixers(n):
                if n == 3:
                    act_e.wait_ge(S("s5_landed"), 16 * 11)
                    run("s5_dt", s5v("dt"), s5_in[:, 2, :], ACT.Exp)
                    act_e.wait_ge(S("s5_lrdt"), 1)
                    run("s5_mag", s5v("mag"), s5v("t1"), ACT.Exp)
                    act_e.wait_ge(S("s5_r"), 1)
                    run("s5_sin", s5v("sin"), s5v("r"), ACT.Sin)
                    run("s5_absr", s5v("t2"), s5v("r"), ACT.Abs)
                    run("s5_cos", s5v("cos"), s5v("t2"), ACT.Sin, scale=-1.0, bias=half_pi[:, 0:1])
                    c_im = s5_cT[:, 1, :, :, :].rearrange("p s a c -> p (s a c)")
                    run("s5_cT_signed", c_im, c_im, ACT.Copy, scale=-1.0)
                if n == 4:
                    act_e.wait_ge(S("norm1_var"), 1)
                    run("norm1_root", root[:, :], var[:, :], ACT.Sqrt)
                if n == 7:
                    wait_product(act_e, "s5_bT")
                    taken(act_e.activation(s5_bT[:, :, :, :].rearrange("p r c s -> p (r c s)"), product("s5_bT")[:, :], ACT.Copy), "s5_bT")
                if n == 9:
                    act_e.wait_ge(tile_scaled, CT * (HG_F + 1))
                    f = flat(HG_FF)
                    run("hg_abs", T[0], f, ACT.Abs)
                    run("hg_exp", T[0], T[0], ACT.Exp, scale=-1.0)
                    run("hg_ln", T[0], T[0], ACT.Ln, bias=1.0)
                    act_e.wait_ge(S("hg_sp"), 1)
                    run("hg_k", T[2], T[2], ACT.Exp, scale=-1.0)
                for k in range(1, LEVELS + 1):
                    if n == AT[f"lev{k}"]:
                        if k == 1:
                            act_e.wait_ge(S("hg_lf"), 1)
                            act_e.wait_ge(S("hg_ex0"), 1)
                        else:
                            act_e.wait_ge(S("hg_segments"), 2 * (k - 1))
                        if k > 2:
                            wait_product(act_e, f"lev{k - 2}")
                        W = halves(T4[4 + k % 2], 2 ** (k - 1))
                        act_e.activation(W[1], halves(T4[1], 2 ** (k - 1))[1], ACT.Exp).then_inc(S("hg_decay"), 1)
                        act_e.activation(W[0], halves(T4[3], 2 ** (k - 1))[0], ACT.Exp).then_inc(S("hg_decay"), 1)
                if n == AT["hg_vT"] + 1:
                    wait_product(act_e, "hg_vT")
                    taken(act_e.activation(flat(HG_FF), product("hg_vT")[:, :], ACT.Copy), "hg_vT")
                if n == AT["hg_o"] + 1:
                    wait_product(act_e, "hg_o")
                    run("hg_o_out", flat(HG_II), product("hg_o")[:, :], ACT.Copy)
                    taken(act_e.activation(T[1], product("hg_o")[:, :], ACT.Square), "hg_o")
                    act_e.wait_ge(tile_scaled, CT * (HG_G + 1))
                    run("hg_sig", T[5], flat(HG_GG), ACT.Sigmoid)
                if n == AT["hg_ss"] + 1:
                    act_e.wait_ge(S("hg_var"), 1)
                    run("hg_root", T[3], T[2], ACT.Sqrt)
                if n == AT["q_ss"]:
                    act_e.wait_ge(tile_scaled, CT * (SB_K + 1))
                    wait_product(act_e, "hg_ss")
                    run("q_sq", T[0], flat(SQ), ACT.Square)
                    run("k_sq", T[1], flat(SK), ACT.Square)
                if n == AT["q_ss"] + 1:
                    act_e.wait_ge(S("q_var"), 1)
                    run("q_root", T[3], T[2], ACT.Sqrt)
                if n == AT["sb_vT"] + 1:
                    act_e.wait_ge(S("k_var"), 1)
                    run("k_root", T[6], T[5], ACT.Sqrt)
                    wait_product(act_e, "sb_vT")
                    taken(act_e.activation(flat(HG_QQ), product("sb_vT")[:, :], ACT.Copy), "sb_vT")
                if n == AT["z0"] + 1:
                    for hh in range(2):
                        wait_product(act_e, f"z{hh}")
                        taken(act_e.activation(Z[:, 768 * hh:768 * (hh + 1)], product(f"z{hh}")[:, 0:768], ACT.Copy), f"z{hh}")
                    for hh in range(2):
                        wait_taken(act_e, f"z{hh}")
                    run("sb_abs", LOG1P, Z, ACT.Abs)
                    run("sb_exp", LOG1P, LOG1P, ACT.Exp, scale=-1.0)
                    run("sb_ln", LOG1P, LOG1P, ACT.Ln, bias=1.0)
                if n == AT["within0"] + 1:
                    for hh in range(2):
                        wait_taken(act_e, f"within{hh}")
                    run("sb_wexp", Z, Z, ACT.Exp)
                if n == AT["sb_o"] + 1:
                    wait_product(act_e, "sb_o")
                    taken(act_e.activation(flat(HG_II), product("sb_o")[:, :], ACT.Copy), "sb_o")
                for g in range(4):
                    if n == 42 + 6 * g:
                        act_e.wait_ge(S("s5_phase"), 3 * (g + 1))
                        cos, sin = s5_tables(g)
                        run("s5_table", flat(sin), flat(cos), ACT.Sin, scale=6.283185)
                        run("s5_table", flat(cos), flat(cos), ACT.Abs)
                        run("s5_table", flat(cos), flat(cos), ACT.Sin, scale=-6.283185, bias=half_pi[:, 0:1])
                if n == 70:
                    act_e.wait_ge(S("s5_y"), CT)
                    act_e.wait_ge(S("s5_x"), 16)
                    run("gelu_sq", T[4], flat(UU), ACT.Square)
                if n == 71:
                    act_e.wait_ge(S("gelu_arg"), 2)
                    run("gelu_sig", T[4], T[4], ACT.Sigmoid, scale=1.5957691216057308)
                if n == 72:
                    act_e.wait_ge(S("gelu"), 1)
                    wait_product(act_e, "s5_y3")
                    run("glu_in_hi", glu_in[:, :, 0, :], UU, ACT.Copy)
                if n == 74:
                    act_e.wait_ge(S("hg_out"), HEADS)
                    run("o_hi", o_hg[:, :, 0, :], HG_GG, ACT.Copy)
                    wait_taken(act_e, "sb_o")
                    run("o_hi", o_sb[:, :, 0, :], HG_II, ACT.Copy)
                for b in range(11):
                    if n == 4 * b + 39:
                        sigmoid_gates(b)

            act_e.dma_start(gain_mix[:, :], norm_mix).then_inc(S("gains_landed"), 16)
            for k in range(4):
                act_e.wait_ge(S(f"x_landed{k}"), 16)
                if k == 0:
                    act_e.wait_ge(S("gains_landed"), 16)
                for c in range(4 * k, 4 * k + 4):
                    act_e.activation(a_in[:, c, 0, :], x_first[:, c, :], ACT.Copy, scale=gain_mix[:, c:c + 1]).then_inc(S("a_in_hi"), 1)
                hi(0, RING, k)
            for q in range(4):
                act_e.activation(squares[:, 4 * q:4 * q + 4, :], x_first[:, 4 * q:4 * q + 4, :], ACT.Square).then_inc(S("x_sq"), 1)

            for n in range(IN_TILES):
                for p in (2 * n + 4, 2 * n + 5):
                    hi(0, RING, p)
                copy_half(n, n, piece_used, 2 * n + 2)
                mixers(n + 1)

            for m in range(CT):
                hi(0, RING, BR_P + m, PIECE if m % 2 == 0 else CT)
                copy_half(GLU_T + 2 * m, 2 * m, S("glu_first"), m + 1)
                copy_half(GLU_T + 2 * m + 1, 2 * m + 1, piece_used, GLU_P + m + 1)
            act_e.wait_ge(tile_summed, BR_T)
            run("glu_sig", flat(HG_QQ), flat(HG_QQ), ACT.Sigmoid)
            sigmoid_gates(11)
            act_e.wait_ge(S("glu_out"), 1)
            run("o_hi", o_s5[:, :, 0, :], HG_FF, ACT.Copy)

            def merged_hi(u, j):
                act_e.wait_ge(S("merged"), u + 1)
                act_e.activation(a_in[:, u, 0, :], merged[:, j % 2, :], ACT.Copy).then_inc(S("merged_hi"), 1)

            def branches(i, last):
                for j in range(RING):
                    for c in range(2):
                        if last and j >= 2:
                            hi(0, RING, OUT_P + 2 * (j - 2) + c)
                        else:
                            hi(i, 2 * RING, BR_P + 2 * (j + 2) + c, PIECE if c == 0 else CT)
                    for b in range(3):
                        n = i * (3 * RING) + (BR_T + 3 * j + b)
                        done, value = ((S("br_first"), i * RING + (j + 1)) if b == 0 else
                                       (piece_used, i * (2 * RING) + (BR_P + 2 * j + b)))
                        copy_half(n, 3 * j + b, done, value)
                    if not (isinstance(i, int) and i == 0 and j == 0):
                        merged_hi(i * RING + (j - 1), j - 1)

            branches(0, False)
            with act_e.Fori(1, KT // RING - 1) as i:
                branches(i, False)
            branches(KT // RING - 1, True)
            merged_hi(KT - 1, KT - 1)

            def outs(i, last):
                for j in range(BANKS):
                    for c in range(2):
                        if last and j >= 2:
                            hi(0, RING, UP_P + 2 * (j - 2) + c)
                        else:
                            hi(i, 2 * BANKS, OUT_P + 2 * (j + 2) + c)
                    copy_half(i * BANKS + (OUT_T + j), j, piece_used, i * (2 * BANKS) + (OUT_P + 2 * j + 2))
                    act_e.wait_ge(S("x1_ready"), i * BANKS + (j + 1))
                    t = i * BANKS + j
                    act_e.activation(h2[:, t, 0, :], x1[:, t, :], ACT.Copy, scale=gain_ffn[:, bass.ds(t, 1)]).then_inc(S("h2_hi"), 1)

            with act_e.Fori(0, OUT_TILES // BANKS - 1) as i:
                outs(i, False)
            outs(OUT_TILES // BANKS - 1, True)

            def tap2(t, j):
                act_e.wait_ge(S("up_scaled"), t + 1)
                if not (isinstance(t, int) and t < 4):
                    act_e.wait_ge(S("act_lo"), (t - 2) // 2 if isinstance(t, int) else conv_base(t, j))
                act_e.activation(convd[:, j % 4, :], padded[:, j % 2, 2:], ACT.Copy, scale=taps[:, t, 2:3]).then_inc(S("tap2"), 1)

            def ups(i, last):
                for j in range(BANKS):
                    first = isinstance(i, int) and i == 0
                    t = i * BANKS + j
                    if j % 2 == 1 and not (first and j < 3):
                        q = i * 2 + (j - 3) // 2
                        act_e.wait_ge(S("conv_done"), t - 1)
                        act_e.activation(silu[:, :], convd[:, (j - 3) % 4, :], ACT.Silu).then_inc(S("silu_done"), 1)
                    for c in range(2):
                        if last and j >= 2:
                            hi(0, RING, DOWN_P + 2 * (j - 2) + c)
                        else:
                            hi(i, 2 * BANKS, UP_P + 2 * (j + 2) + c)
                    if first and j == 1:
                        act_e.wait_ge(S("norm2_var"), 1)
                        run("norm2_root", root[:, :], var[:, :], ACT.Sqrt)
                    copy_half(i * BANKS + (UP_T + j), j, piece_used, i * (2 * BANKS) + (UP_P + 2 * j + 2))
                    if not (first and j == 0):
                        tap2_at(i, j - 1)
                    if j % 2 == 1 and not (first and j < 3):
                        hidden_hi(q, j)

            def tap2_at(i, j):
                t = i * BANKS + j
                act_e.wait_ge(S("up_scaled"), t + 1)
                if not (isinstance(i, int) and t < 4):
                    act_e.wait_ge(S("act_lo"), i * 2 + (j // 2 - 1))
                act_e.activation(convd[:, j % 4, :], padded[:, j % 2, 2:], ACT.Copy, scale=taps[:, t, 2:3]).then_inc(S("tap2"), 1)

            def hidden_hi(q, j):
                act_e.wait_ge(S("hidden"), q + 1)
                act_e.activation(act[:, q, 0, :], convd[:, (j - 2) % 4, :], ACT.Copy).then_inc(S("act_hi"), 1)

            ups(0, False)
            with act_e.Fori(1, UP_TILES // BANKS - 1) as i:
                ups(i, False)
            ups(UP_TILES // BANKS - 1, True)
            tap2_at(UP_TILES // BANKS, -1)
            act_e.wait_ge(S("conv_done"), UP_TILES)
            act_e.activation(silu[:, :], convd[:, 2, :], ACT.Silu).then_inc(S("silu_done"), 1)
            hidden_hi(FT - 1, 1)

            def downs(i, last):
                n_p = len(DOWN_PIECES)
                for j in range(BANKS):
                    for c in range(n_p):
                        p = j * n_p + RING + c
                        if not last or p < BANKS * n_p:
                            hi(i, BANKS * n_p, DOWN_P + p, DOWN_PIECES[p % n_p])
                    copy_half(i * BANKS + (DOWN_T + j), j, piece_used, i * (BANKS * n_p) + (DOWN_P + n_p * (j + 1)))

            with act_e.Fori(0, DOWN_TILES // BANKS - 1) as i:
                downs(i, False)
            downs(DOWN_TILES // BANKS - 1, True)

        @block.vector
        def _(ve):
            def lo(i, per, p0, blocks=PIECE):
                p, s = i * per + p0, p0 % RING
                ve.wait_ge(hi_ready, p + 1)
                w = slice(0, blocks * P)
                ve.tensor_tensor(w_lo[s][:, w], raw[s][:, w], w_hi[s][:, w].bitcast(F32), ALU.subtract).then_inc(lo_ready, 1)

            def add_halves(n, j, dest):
                ve.wait_ge(half_copied, n + 1)
                ve.tensor_tensor(dest, bank[j % BANKS][:, 0:SEQ], half[j % 2][:, :], ALU.add).then_inc(tile_summed, 1)

            def tt(name, out_, a, b, op):
                link(ve, ve.tensor_tensor(out_, a, b, op), name)

            def ts(name, out_, a, s1, s2, op0, op1=None):
                ins = ve.tensor_scalar(out_, a, s1, None, op0) if op1 is None else ve.tensor_scalar(out_, a, s1, s2, op0, op1)
                link(ve, ins, name)

            def stt(name, out_, a, s_, b, op0, op1):
                link(ve, ve.scalar_tensor_tensor(out_, a, s_, b, op0, op1), name)

            def inverse_root(name, v, y, t):
                ve.wait_ge(S(name + "_root"), 1)
                link(ve, ve.reciprocal(y, y), name + "_newton")
                tt(name + "_newton", t, y, y, ALU.mult)
                stt(name + "_newton", t, t, -0.5, v, ALU.mult, ALU.mult)
                stt(name + "_rstd", y, t, 1.5, y, ALU.add, ALU.mult)

            def mean(name, out_, of):
                wait_product(ve, name)
                n_feat = D_MODEL if name.startswith("norm") else P
                taken(ve.tensor_scalar(out_, product(name)[:, 0:of], 1.0 / n_feat, EPS, ALU.mult, ALU.add), name)
                wait_taken(ve, name)

            def s5_setup():
                lr, li = s5_in[:, 0, :], s5_in[:, 1, :]
                c = "s5_setup"
                ve.wait_ge(S("s5_dt"), 1)
                tt("s5_lrdt", s5v("t1"), lr, s5v("dt"), ALU.mult)
                tt(c, s5v("theta"), li, s5v("dt"), ALU.mult)
                ts(c, s5v("t3"), s5v("theta"), 1.0 / TWO_PI, MAGIC, ALU.mult, ALU.add)
                ts(c, s5v("t3"), s5v("t3"), MAGIC, None, ALU.subtract)
                stt(c, s5v("theta"), s5v("t3"), -TWO_PI_HI, s5v("theta"), ALU.mult, ALU.add)
                stt(c, s5v("theta"), s5v("t3"), -(TWO_PI - TWO_PI_HI), s5v("theta"), ALU.mult, ALU.add)
                ts(c, s5v("turns"), s5v("theta"), 1.0 / TWO_PI, None, ALU.mult)
                ts("s5_r", s5v("r"), s5v("theta"), BELOW_PI, -BELOW_PI, ALU.min, ALU.max)
                ve.wait_ge(S("s5_cos"), 1)
                ve.wait_ge(S("s5_mag"), 1)
                tt(c, s5v("cos"), s5v("cos"), s5v("mag"), ALU.mult)
                ts(c, s5v("cos"), s5v("cos"), 1.0, None, ALU.subtract)
                tt(c, s5v("sin"), s5v("sin"), s5v("mag"), ALU.mult)
                tt(c, s5v("t1"), lr, lr, ALU.mult)
                tt(c, s5v("t2"), li, li, ALU.mult)
                tt(c, s5v("t1"), s5v("t1"), s5v("t2"), ALU.add)
                link(ve, ve.reciprocal(s5v("t3"), s5v("t1")), c)
                tt(c, s5v("t1"), s5v("cos"), lr, ALU.mult)
                tt(c, s5v("t2"), s5v("sin"), li, ALU.mult)
                tt(c, s5v("t1"), s5v("t1"), s5v("t2"), ALU.add)
                tt(c, s5v("zr"), s5v("t1"), s5v("t3"), ALU.mult)
                tt(c, s5v("t1"), s5v("sin"), lr, ALU.mult)
                tt(c, s5v("t2"), s5v("cos"), li, ALU.mult)
                tt(c, s5v("t1"), s5v("t1"), s5v("t2"), ALU.subtract)
                tt(c, s5v("zi"), s5v("t1"), s5v("t3"), ALU.mult)
                b = T[0].rearrange("p (r s c) -> p r s c", r=4, c=S5_CH)
                full = [P, ST, S5_CH]
                zr, zi = (bc(s5v(x).unsqueeze(2), full) for x in ("zr", "zi"))
                out_ = T[1].rearrange("p (r s g c) -> p r s g c", r=2, s=ST, g=2)
                for r, (x, y, op) in enumerate(((0, 1, ALU.subtract), (1, 0, ALU.add))):
                    tt(c, b[:, 2], b[:, x], zr, ALU.mult)
                    tt(c, b[:, 3], b[:, y], zi, ALU.mult)
                    for g in range(2):
                        rows = slice(64 * g, 64 * g + 64)
                        tt("s5_bb", out_[rows, r, :, g, :], b[rows, 2], b[rows, 3], op)

            def mixers(n):
                if n == 3:
                    s5_setup()
                if n == 4:
                    mean("norm1", var[:, :], SEQ)
                    ve.sem_inc(S("norm1_var"), 1) if False else ve.nop().then_inc(S("norm1_var"), 1)
                    ve.wait_ge(S("norm1_root"), 1)
                    link(ve, ve.reciprocal(root[:, :], root[:, :]), "norm1_newton")
                    tt("norm1_newton", rstd[:, :], root[:, :], root[:, :], ALU.mult)
                    stt("norm1_newton", rstd[:, :], rstd[:, :], -0.5, var[:, :], ALU.mult, ALU.mult)
                    stt("norm1_rstd", rstd[:, :], rstd[:, :], 1.5, root[:, :], ALU.add, ALU.mult)
                if n == 9:
                    ve.wait_ge(S("hg_ln"), 1)
                    f = flat(HG_FF)
                    stt("hg_sp", T[2], f, 0.0, T[0], ALU.max, ALU.add)
                    stt("hg_lf", T[1], f, 0.0, T[0], ALU.min, ALU.subtract)
                    link(ve, ve.memset(T[3], 0.0), "hg_ex0")
                for k in range(1, LEVELS + 1):
                    if n == AT[f"lev{k}"]:
                        W = halves(T4[4 + k % 2], 2 ** (k - 1))
                        ve.wait_ge(S("hg_decay"), 2 * k)
                        ve.tensor_tensor(W[1], W[1], halves(HG_QQ, 2 ** (k - 1))[1], ALU.mult).then_inc(S("hg_factors"), 1)
                        ve.tensor_tensor(W[0], W[0], halves(T4[2], 2 ** (k - 1))[0], ALU.mult).then_inc(S("hg_factors"), 1)
                full = [P, 8, P]
                for k in range(LEVELS + 1):
                    if n == AT[f"lev{k}"] + 1:
                        wait_product(ve, f"lev{k}")
                        ps = product(f"lev{k}").rearrange("p (s t) -> p s t", t=P)
                        if k == 0:
                            ins = ve.tensor_tensor(T2[6], ps, bc(eye[:, :].unsqueeze(1), full), ALU.mult)
                        elif k < LEVELS:
                            ins = ve.copy_predicated(T2[6], bc(level_mask[:, k:k + 1, :], full), ps)
                        else:
                            ins = ve.tensor_copy(T[0][:, 0:512], product("lev8")[:, 0:512])
                        taken(ins, f"lev{k}")
                        wait_taken(ve, f"lev{k}")
                if n == AT["hg_ss"] + 1:
                    mean("hg_ss", T[2], 1024)
                    ve.nop().then_inc(S("hg_var"), 1)
                    inverse_root("hg", T[2], T[3], T[4])
                if n == AT["hg_ss"] + 2:
                    ve.wait_ge(S("hg_sig"), 1)
                    tt("hg_norm", flat(HG_GG), flat(HG_GG), T[5], ALU.mult)
                    tt("hg_norm", flat(HG_II), flat(HG_II), T[3], ALU.mult)
                    for c in range(HEADS):
                        stt("hg_out", HG_GG[:, c, :], HG_II[:, c, :], gain_hg[:, c:c + 1], HG_GG[:, c, :], ALU.mult, ALU.mult)
                if n == AT["q_ss"] + 1:
                    mean("q_ss", T[2], 1024)
                    ve.nop().then_inc(S("q_var"), 1)
                    mean("k_ss", T[5], 1024)
                    ve.nop().then_inc(S("k_var"), 1)
                    inverse_root("q", T[2], T[3], T[4])
                    ts("sb_gain", gain_sb[:, 0:1], gain_sb[:, 0:1], P ** -0.5, None, ALU.mult)
                    stt("q_normed", flat(SQ), flat(SQ), gain_sb[:, 0:1], T[3], ALU.mult, ALU.mult)
                if n == AT["sb_vT"] + 1:
                    inverse_root("k", T[5], T[6], T[4])
                    stt("k_normed", flat(SK), flat(SK), gain_sb[:, 1:2], T[6], ALU.mult, ALU.mult)

                def causal(name, x):
                    for hh in range(2):
                        for at, step in ((0, SEQ), (512, P)):
                            v = x[:, 768 * hh + at:768 * hh + at + 2 * step].rearrange("p (i t) -> p i t", i=2)[:, :, 0:P]
                            tt(name, v, v, bc(upper[:, :].unsqueeze(1), [P, 2, P]), ALU.mult)

                if n == AT["z0"] + 1:
                    ve.wait_ge(S("sb_ln"), 1)
                    stt("sb_sp", SOFTP, Z, 0.0, LOG1P, ALU.max, ALU.add)
                    stt("sb_ls", Z, Z, 0.0, LOG1P, ALU.min, ALU.subtract)
                    causal("sb_masked", SOFTP)
                if n == AT["within0"] + 1:
                    for hh in range(2):
                        wait_product(ve, f"within{hh}")
                        z = Z[:, 768 * hh:768 * (hh + 1)]
                        taken(ve.tensor_tensor(z, z, product(f"within{hh}")[:, 0:768], ALU.subtract), f"within{hh}")
                    ve.wait_ge(S("sb_wexp"), 1)
                    causal("sb_w", Z)
                for k in range(8):
                    if n == AT[f"bu{k}"] + 1:
                        wait_product(ve, f"bu{k}")
                        ve.wait_ge(S("s5_table"), 3 * (k // 2 + 1))
                        if k >= 2:
                            ve.wait_ge(S("s5_x"), 2 * (k - 1))
                        cos, sin = (t[:, s5_slice(k), :] for t in s5_tables(k // 2))
                        bu = product(f"bu{k}").rearrange("p (i r t) -> p r i t", i=2, r=2)
                        re, im = bu[:, 0], bu[:, 1]
                        y_re, y_im, t0, t1 = T4[4][:, s5_slice(k), :], T4[5][:, s5_slice(k), :], T4[6][:, 0:2, :], T4[6][:, 2:4, :]
                        tt("s5_rot", y_re, re, cos, ALU.mult)
                        tt("s5_rot", t0, im, sin, ALU.mult)
                        tt("s5_rot", y_im, im, cos, ALU.mult)
                        taken(ve.tensor_tensor(t1, re, sin, ALU.mult), f"bu{k}")
                        wait_taken(ve, f"bu{k}")
                        tt("s5_rot", y_re, y_re, t0, ALU.add)
                        tt("s5_rot", y_im, y_im, t1, ALU.subtract)
                        for y in (y_re, y_im):
                            for i in range(2):
                                v = y[:, i, :]
                                link(ve, ve.tensor_tensor_scan(v, bc(s5v("mag")[:, 2 * k + i:2 * k + i + 1], [P, SEQ]), v,
                                                               0.0, ALU.mult, ALU.add), "s5_scan")
                for c in range(CT):
                    if n == AT[f"s5_y{c}"] + 1:
                        wait_product(ve, f"s5_y{c}")
                        ins = ve.scalar_tensor_tensor(UU[:, c, :], UU[:, c, :], skip_s5[:, c:c + 1], product(f"s5_y{c}")[:, 0:SEQ],
                                                      ALU.mult, ALU.add)
                        taken(ins, f"s5_y{c}")
                        wait_taken(ve, f"s5_y{c}")
                        ve.nop().then_inc(S("s5_y"), 1)
                if n == 70:
                    ve.wait_ge(S("gelu_sq"), 1)
                    ts("gelu_arg", T[4], T[4], 0.044715, 1.0, ALU.mult, ALU.add)
                    tt("gelu_arg", T[4], T[4], flat(UU), ALU.mult)
                if n == 71:
                    ve.wait_ge(S("gelu_sig"), 1)
                    tt("gelu", flat(UU), flat(UU), T[4], ALU.mult)
                if n == 72:
                    ve.wait_ge(S("glu_in_hi"), 1)
                    tt("glu_in_lo", glu_in[:, :, 1, :], UU, glu_in[:, :, 0, :].bitcast(F32), ALU.subtract)
                if n == 74:
                    for m, (o, x) in enumerate(((o_hg, HG_GG), (o_sb, HG_II))):
                        ve.wait_ge(S("o_hi"), m + 1)
                        tt("o_split", o[:, :, 1, :], x, o[:, :, 0, :].bitcast(F32), ALU.subtract)

            ve.wait_ge(S("iota"), 3)
            diff, xor = T[4][:, 0:P].bitcast(I32), T[4][:, P:2 * P].bitcast(I32)
            row = T[4][:, 2 * P:3 * P].bitcast(I32)
            link(ve, ve.memset(half_pi[:, :], TWO_PI / 4), "masks")
            link(ve, ve.tensor_tensor(xor, xor, row, ALU.bitwise_xor), "masks")
            ts("masks", eye[:, :], diff, 0.0, None, ALU.is_equal)
            ts("masks", upper[:, :], diff, 0.0, None, ALU.is_gt)
            ts("masks", lower[:, :], diff, 0.0, None, ALU.is_lt)
            for k in range(1, LEVELS):
                stt("masks", level_mask[:, k, :], xor, float(2 ** (k - 1)), upper[:, :], ALU.is_ge, ALU.mult)

            for k in range(4):
                for c in range(4 * k, 4 * k + 4):
                    ve.wait_ge(S("a_in_hi"), c + 1)
                    ve.scalar_tensor_tensor(a_in[:, c, 1, :], x_first[:, c, :], gain_mix[:, c:c + 1], a_in[:, c, 0, :].bitcast(F32),
                                            ALU.mult, ALU.subtract).then_inc(S("a_in_lo"), 1)
                lo(0, RING, k)

            for n in range(IN_TILES):
                for p in (2 * n + 4, 2 * n + 5):
                    lo(0, RING, p)
                add_halves(n, n, proj(n))
                mixers(n + 1)

            for m in range(CT):
                lo(0, RING, BR_P + m, PIECE if m % 2 == 0 else CT)
                add_halves(GLU_T + 2 * m, 2 * m, HG_FF[:, m, :])
                add_halves(GLU_T + 2 * m + 1, 2 * m + 1, HG_QQ[:, m, :])
            ve.wait_ge(S("glu_sig"), 1)
            tt("glu_out", flat(HG_FF), flat(HG_FF), flat(HG_QQ), ALU.mult)
            ve.wait_ge(S("o_hi"), 3)
            tt("o_split", o_s5[:, :, 1, :], HG_FF, o_s5[:, :, 0, :].bitcast(F32), ALU.subtract)

            def merged_lo(u, j):
                ve.wait_ge(S("merged_hi"), u + 1)
                ve.tensor_tensor(a_in[:, u, 1, :], merged[:, j % 2, :], a_in[:, u, 0, :].bitcast(F32), ALU.subtract)\
                    .then_inc(S("merged_lo"), 1)

            def branches(i, last):
                first = isinstance(i, int) and i == 0
                for j in range(RING):
                    for c in range(2):
                        if last and j >= 2:
                            lo(0, RING, OUT_P + 2 * (j - 2) + c)
                        else:
                            lo(i, 2 * RING, BR_P + 2 * (j + 2) + c, PIECE if c == 0 else CT)
                    for b in range(3):
                        if not (first and 3 * j + b < 4):
                            ve.wait_ge(S("merged"), i * RING + (j - 1 if b == 0 else j))
                        add_halves(i * (3 * RING) + (BR_T + 3 * j + b), 3 * j + b, gated[:, (3 * j + b) % 4, :])
                    if not (first and j == 0):
                        merged_lo(i * RING + (j - 1), j - 1)

            branches(0, False)
            with ve.Fori(1, KT // RING - 1) as i:
                branches(i, False)
            branches(KT // RING - 1, True)
            merged_lo(KT - 1, KT - 1)

            def outs(i, last):
                for j in range(BANKS):
                    for c in range(2):
                        if last and j >= 2:
                            lo(0, RING, UP_P + 2 * (j - 2) + c)
                        else:
                            lo(i, 2 * BANKS, OUT_P + 2 * (j + 2) + c)
                    t = i * BANKS + j
                    add_halves(i * BANKS + (OUT_T + j), j, convd[:, j, :])
                    ve.wait_ge(tile_summed, i * BANKS + (OUT_T + j + 1))
                    ve.wait_ge(S("x1_landed"), 16)
                    ve.tensor_tensor(x1[:, t, :], x1[:, t, :], convd[:, j, :], ALU.add).then_inc(S("x1_ready"), 1)
                    ve.wait_ge(S("h2_hi"), i * BANKS + (j + 1))
                    ve.scalar_tensor_tensor(h2[:, t, 1, :], x1[:, t, :], gain_ffn[:, bass.ds(t, 1)], h2[:, t, 0, :].bitcast(F32),
                                            ALU.mult, ALU.subtract).then_inc(S("h2_lo"), 1)

            with ve.Fori(0, OUT_TILES // BANKS - 1) as i:
                outs(i, False)
            outs(OUT_TILES // BANKS - 1, True)

            def conv(i, j):
                t = i * BANKS + j
                ve.wait_ge(S("tap2"), t + 1)
                c = convd[:, j % 4, :]
                ve.scalar_tensor_tensor(c, padded[:, j % 2, 1:SEQ + 1], taps[:, t, 1:2], c, ALU.mult, ALU.add).then_inc(S("tap1"), 1)
                ve.wait_ge(S("tap1"), t + 1)
                ve.scalar_tensor_tensor(c, padded[:, j % 2, 0:SEQ], taps[:, t, 0:1], c, ALU.mult, ALU.add).then_inc(S("conv_done"), 1)

            def hidden(q, j):
                ve.wait_ge(S("silu_done"), q + 1)
                c = convd[:, (j - 2) % 4, :]
                ve.tensor_tensor(c, silu[:, :], c, ALU.mult).then_inc(S("hidden"), 1)

            def hidden_lo(q, j):
                ve.wait_ge(S("act_hi"), q + 1)
                ve.tensor_tensor(act[:, q, 1, :], convd[:, (j - 2) % 4, :], act[:, q, 0, :].bitcast(F32), ALU.subtract)\
                    .then_inc(S("act_lo"), 1)

            def ups(i, last):
                first = isinstance(i, int) and i == 0
                for j in range(BANKS):
                    pair_due = j % 2 == 1 and not (first and j < 3)
                    q = i * 2 + (j - 3) // 2
                    for c in range(2):
                        if last and j >= 2:
                            lo(0, RING, DOWN_P + 2 * (j - 2) + c)
                        else:
                            lo(i, 2 * BANKS, UP_P + 2 * (j + 2) + c)
                        if first and j == 0 and c == 0:
                            pass
                    if first and j == 1:
                        mean("norm2", var[:, :], SEQ)
                        ve.nop().then_inc(S("norm2_var"), 1)
                        ve.wait_ge(S("norm2_root"), 1)
                        link(ve, ve.reciprocal(root[:, :], root[:, :]), "norm2_newton")
                        tt("norm2_newton", rstd[:, :], root[:, :], root[:, :], ALU.mult)
                        stt("norm2_newton", rstd[:, :], rstd[:, :], -0.5, var[:, :], ALU.mult, ALU.mult)
                        stt("norm2_rstd", rstd[:, :], rstd[:, :], 1.5, root[:, :], ALU.add, ALU.mult)
                    if not (first and j < 2):
                        ve.wait_ge(S("up_scaled"), i * BANKS + (j - 1))
                    add_halves(i * BANKS + (UP_T + j), j, sum_u[:, j % 2, :])
                    if pair_due:
                        hidden(q, j)
                    if not (first and j == 0):
                        conv(i, j - 1)
                    if pair_due:
                        hidden_lo(q, j)

            ups(0, False)
            with ve.Fori(1, UP_TILES // BANKS - 1) as i:
                ups(i, False)
            ups(UP_TILES // BANKS - 1, True)
            conv(UP_TILES // BANKS, -1)
            hidden(FT - 1, 1)
            hidden_lo(FT - 1, 1)

            def downs(i, last):
                n_p = len(DOWN_PIECES)
                for j in range(BANKS):
                    for c in range(n_p):
                        p = j * n_p + RING + c
                        if not last or p < BANKS * n_p:
                            lo(i, BANKS * n_p, DOWN_P + p, DOWN_PIECES[p % n_p])
                    t = i * BANKS + j
                    add_halves(i * BANKS + (DOWN_T + j), j, convd[:, j, :])
                    ve.wait_ge(tile_summed, i * BANKS + (DOWN_T + j + 1))
                    ve.tensor_tensor(x1[:, t, :], x1[:, t, :], convd[:, j, :], ALU.add).then_inc(S("y_ready"), 1)

            with ve.Fori(0, DOWN_TILES // BANKS - 1) as i:
                downs(i, False)
            downs(DOWN_TILES // BANKS - 1, True)

        @block.gpsimd
        def _(pool):
            def tt(name, out_, a, b, op):
                link(pool, pool.tensor_tensor(out_, a, b, op), name)

            b = T[0].rearrange("p (r x) -> p r x", r=4)
            pool.dma_start(s5_in[:, :, :], s5_small).then_inc(S("s5_landed"), 16)
            pool.dma_start(b[:, 0:2, :], s5_b).then_inc(S("s5_landed"), 16)
            link(pool, pool.memset(s5_cT[:, :, :, :, :], 0.0), "s5_zero")
            for r in range(2):
                for g in range(2):
                    pool.dma_start(s5_cT[64 * g:64 * g + 64, r, :, g, :], s5_c[64 * g:64 * g + 64, r, :, :]).then_inc(S("s5_landed"), 16)
            for dst, src in ((gain_ffn, norm_ffn), (gain_hg, hg_gain), (gain_sb, sb_gain), (skip_s5, s5_skip)):
                pool.dma_start(dst[:, :], src).then_inc(S("s5_landed"), 16)
            pool.dma_start(taps[:, :, :], conv).then_inc(S("s5_landed"), 16)
            link(pool, pool.memset(ones[:, :], 1.0), "ones")
            link(pool, pool.memset(T[1], 0.0), "s5_zero")
            ints = T[4].bitcast(I32)
            for c, (step, mult) in enumerate(((1, -1), (1, 0), (0, 1))):
                link(pool, pool.iota(ints[:, c * P:(c + 1) * P], [[step, P]], base=0, channel_multiplier=mult), "iota")
            link(pool, pool.iota(T[5][:, 0:SEQ].bitcast(I32), [[1, SEQ]], base=0, channel_multiplier=0), "time_i")
            link(pool, pool.tensor_copy(time_f[:, :], T[5][:, 0:SEQ].bitcast(I32)), "time_f")

            pool.wait_ge(S("x_sq"), 4)
            for m in (8, 4, 2, 1):
                tt("x_sq_sum", squares[:, 0:m, :], squares[:, 0:m, :], squares[:, m:2 * m, :], ALU.add)

            def scale(n):
                if n == 0:
                    pool.wait_ge(S("norm1_rstd"), 1)
                pool.wait_ge(tile_summed, n + 1)
                pool.tensor_tensor(proj(n), proj(n), rstd[:, :], ALU.mult).then_inc(tile_scaled, 1)

            def mixers(n):
                for k in range(1, LEVELS):
                    if n == AT[f"lev{k}"]:
                        pool.wait_ge(S("hg_decay"), 2 * k)
                        h = 2 ** (k - 1)
                        pre, suf = halves(T4[1], h), halves(T4[3], h)
                        shape = [P, 1024 // (2 * h), h]
                        tt("hg_segments", suf[0], suf[0], bc(pre[1][:, :, h - 1:h], shape), ALU.add)
                        tt("hg_segments", pre[1], pre[1], bc(pre[0][:, :, h - 1:h], shape), ALU.add)
                for g in range(4):
                    if n == 41 + 6 * g:
                        cos, sin = s5_tables(g)
                        if g == 0:
                            pool.wait_ge(S("sb_ls"), 1)
                        if g == 1:
                            wait_product(pool, "sb_o")
                        tt("s5_phase", cos, bc(time_f[:, :].unsqueeze(1), [P, 4, SEQ]),
                           bc(s5v("turns")[:, 4 * g:4 * g + 4].unsqueeze(2), [P, 4, SEQ]), ALU.mult)
                        link(pool, pool.tensor_scalar(flat(sin), flat(cos), MAGIC, MAGIC, ALU.add, ALU.subtract), "s5_phase")
                        tt("s5_phase", flat(cos), flat(cos), flat(sin), ALU.subtract)
                for k in range(8):
                    if n == AT[f"bu{k}"] + 2:
                        pool.wait_ge(S("s5_scan"), 4 * (k + 1))
                        c = k // 2
                        if k % 2 == 0 and c > 0:
                            wait_product(pool, f"s5_y{c - 1}")
                        cos, sin = (t[:, s5_slice(k), :].rearrange("p a b -> p (a b)") for t in s5_tables(c))
                        h = slice(512 * (k % 2), 512 * (k % 2) + 512)
                        y_re, y_im = T[4][:, h], T[5][:, h]
                        t0, t1 = (proj1[:, 2, 2 * i:2 * i + 2, :].rearrange("p a b -> p (a b)") for i in range(2))
                        x = [proj1[:, r, s5_slice(k), :].rearrange("p a b -> p (a b)") for r in range(2)]
                        tt("s5_unrot", t0, y_re, cos, ALU.mult)
                        tt("s5_unrot", t1, y_im, sin, ALU.mult)
                        tt("s5_x", x[0], t0, t1, ALU.subtract)
                        tt("s5_unrot", t0, y_re, sin, ALU.mult)
                        tt("s5_unrot", t1, y_im, cos, ALU.mult)
                        tt("s5_x", x[1], t0, t1, ALU.add)

            for n in range(IN_TILES):
                scale(n)
                mixers(n + 1)

            pool.wait_ge(S("o_split"), 3)
            pool.dma_start(x1[:, :, :], xT).then_inc(S("x1_landed"), 16)

            pool.wait_ge(S("gate_ready"), 12)

            def merge(i):
                for j in range(RING):
                    u = i * RING + j
                    for b in range(3):
                        g = gated[:, (3 * j + b) % 4, :]
                        pool.wait_ge(tile_summed, i * (3 * RING) + (BR_T + 3 * j + b + 1))
                        pool.tensor_tensor(g, g, gates[:, i * (3 * RING) + (3 * j + b), :], ALU.mult).then_inc(S("gated"), 1)
                    if not (isinstance(i, int) and i == 0 and j < 2):
                        pool.wait_ge(S("merged_lo"), i * RING + (j - 1))
                    m = merged[:, j % 2, :]
                    pool.wait_ge(S("gated"), i * (3 * RING) + (3 * j + 3))
                    pool.tensor_tensor(m, gated[:, (3 * j) % 4, :], gated[:, (3 * j + 1) % 4, :], ALU.add).then_inc(S("merged2"), 1)
                    pool.wait_ge(S("merged2"), u + 1)
                    pool.tensor_tensor(m, m, gated[:, (3 * j + 2) % 4, :], ALU.add).then_inc(S("merged"), 1)

            merge(0)
            with pool.Fori(1, KT // RING) as i:
                merge(i)

            pool.wait_ge(S("x1_ready"), 1)
            link(pool, pool.tensor_tensor(root[:, :], x1[:, 0, :], x1[:, 0, :], ALU.mult), "x1_sq_sum")
            with pool.Fori(1, KT) as i:
                pool.wait_ge(S("x1_ready"), i + 1)
                pool.tensor_tensor(silu[:, :], x1[:, i, :], x1[:, i, :], ALU.mult).then_inc(S("x1_sq"), 1)
                pool.wait_ge(S("x1_sq"), i)
                pool.tensor_tensor(root[:, :], root[:, :], silu[:, :], ALU.add).then_inc(S("x1_sq_sum"), 1)
                pool.wait_ge(S("x1_sq_sum"), i + 1)

            link(pool, pool.memset(padded[:, :, 0:2], 0.0), "pad_zero")
            pool.wait_ge(S("norm2_rstd"), 1)

            def up_scale(i):
                for j in range(2):
                    t = i * 2 + j
                    pool.wait_ge(tile_summed, i * 2 + (UP_T + j + 1))
                    if not isinstance(i, int):
                        pool.wait_ge(S("conv_done"), t - 1)
                    pool.tensor_tensor(padded[:, j, 2:], sum_u[:, j, :], rstd[:, :], ALU.mult).then_inc(S("up_scaled"), 1)

            up_scale(0)
            with pool.Fori(1, UP_TILES // 2) as i:
                up_scale(i)

            with pool.Fori(0, DOWN_TILES // BANKS - 1) as i:
                pool.wait_ge(S("y_ready"), i * BANKS + BANKS)
                pool.dma_start(out[i, :, :, :], x1[:, bass.ds(i * BANKS, BANKS), :]).then_inc(S("stored"), 16)
            last = DOWN_TILES // BANKS - 1
            for j in range(BANKS):
                pool.wait_ge(S("y_ready"), last * BANKS + j + 1)
                pool.dma_start(out[last, :, j:j + 1, :], x1[:, last * BANKS + j:last * BANKS + j + 1, :]).then_inc(S("stored"), 16)
            pool.wait_ge(S("stored"), 16 * (last + BANKS))


def kernel(**inputs):
    import numpy as np
    import concourse.bacc as bacc
    from concourse.bass_utils import run_bass_kernel_spmd

    a = {k: np.asarray(v) for k, v in inputs.items()}
    width = PIECE * P

    def tiles(w, cols):
        return w.reshape(-1, P, w.shape[1] // P, P).transpose(2, 1, 0, 3)[cols]

    def pieces(w, cols):
        t = tiles(w, cols)
        return np.ascontiguousarray(t.reshape(len(cols), P, 2, width).transpose(0, 2, 1, 3).reshape(-1, P, width))

    def columns(v):
        return np.ascontiguousarray(v.reshape(-1, P).T)

    order = [1, 0, 2, 3, 4, 5, 6, 7]
    in_cols = [CT * g + c for g in order for c in range(CT)]
    in_cols += [8 * CT + KT * b + j for j in range(KT) for b in (0, 2, 1)]
    up_cols = [h * FT + t for t in range(FT) for h in range(2)]
    glu = tiles(a["s5_w_glu"][0], [h * CT + c for c in range(CT) for h in range(2)])
    w_branch = np.stack([tiles(a["w_branch"][0, b], list(range(KT))) for b in (0, 2, 1)], 2)

    def states(v):
        v = v.reshape((ST, P) + v.shape[2:])
        return v.transpose((1, 0) + tuple(range(2, v.ndim)))

    arrays = {
        "xT": a["x"][0].reshape(SEQ, KT, P).transpose(2, 1, 0),
        "w_in": pieces(a["w_in"][0], in_cols),
        "w_glu": glu.reshape(CT, 2, P, CT * P).transpose(0, 2, 1, 3).reshape(CT, P, width),
        "w_br": w_branch.reshape(KT, P, N_BRANCH * CT * P),
        "w_out": pieces(a["w_out"][0], list(range(KT))),
        "w_up": pieces(a["w_up"][0], up_cols),
        "w_down": tiles(a["w_down"][0], list(range(KT))).reshape(KT, P, FT * P),
        "norm_mix": columns(a["norm_mix_g"][0]),
        "norm_ffn": columns(a["norm_ffn_g"][0]),
        "hg_gain": columns(a["hg_norm_g"][0]),
        "s5_small": np.stack([states(a["s5_a_re"][0]), states(a["s5_a_im"][0]),
                              states(np.broadcast_to(a["s5_log_dt"][0][:, None], (S5_GROUPS, S5_STATE)))], 1),
        "s5_b": np.stack([states(a[k][0]).reshape(P, ST * S5_CH) for k in ("s5_b_re", "s5_b_im")], 1),
        "s5_c": np.stack([states(a[k][0].transpose(0, 2, 1)) for k in ("s5_c_re", "s5_c_im")], 1),
        "s5_skip": columns(a["s5_d"][0]),
        "sb_gain": np.stack([a["sb_q_g"][0], a["sb_k_g"][0]], 1),
        "conv": a["conv_w"][0].reshape(3, 2, FT, P).transpose(3, 2, 1, 0).reshape(P, UP_TILES, 3),
    }
    nc = bacc.Bacc("TRN2", target_bir_lowering=False, num_devices=1)
    args = []
    for name, v in arrays.items():
        arrays[name] = v = np.ascontiguousarray(v)
        args.append(nc.dram_tensor(name, v.shape, mybir.dt.from_np(v.dtype), kind="ExternalInput").ap())
    args.append(nc.dram_tensor("out", (KT // BANKS, P, BANKS, SEQ), F32, kind="ExternalOutput").ap())
    layer(nc, **dict(zip(list(arrays) + ["out"], args)))
    r = run_bass_kernel_spmd(nc, [arrays], core_ids=[0])
    got = r.results[0]["out"]
    return np.ascontiguousarray(got.transpose(3, 0, 2, 1).reshape(1, SEQ, D_MODEL))
```

```python
import math
from contextlib import ExitStack

import concourse.bass as bass
from concourse import mybir

F32 = mybir.dt.float32
F32R = mybir.dt.float32r
I32 = mybir.dt.int32
U8 = mybir.dt.uint8
ALU = mybir.AluOpType
ACT = mybir.ActivationFunctionType

P = 128
D_MODEL = 2048
SEQ = 256
BW = D_MODEL // 4
HEADS = BW // P
D_FF = 256 * ((8 * D_MODEL // 3 + 255) // 256)
KT = D_MODEL // P
FT = D_FF // P
CT = BW // P
N_BRANCH = 3
S5_GROUPS, S5_STATE, S5_CH = 32, 64, 16
ST = S5_GROUPS * S5_STATE // P
EPS = 1e-6
LEVELS = 8

HG_F, HG_Q, HG_I, HG_G, S5_U, SB_Q, SB_K, SB_V = range(8)

RING = 4
PIECE = 8
BANKS = 4
DOWN_PIECES = [PIECE] * (FT // PIECE) + [FT % PIECE]

IN_TILES = 8 * CT + N_BRANCH * KT
GLU_TILES = 2 * CT
BR_TILES = N_BRANCH * KT
OUT_TILES = KT
UP_TILES = 2 * FT
DOWN_TILES = KT
GLU_T = IN_TILES
BR_T = GLU_T + GLU_TILES
OUT_T = BR_T + BR_TILES
UP_T = OUT_T + OUT_TILES
DOWN_T = UP_T + UP_TILES
GLU_P = 2 * IN_TILES
BR_P = GLU_P + GLU_TILES // 2
OUT_P = BR_P + 2 * KT
UP_P = OUT_P + 2 * OUT_TILES
DOWN_P = UP_P + 2 * UP_TILES
assert all(x % RING == 0 for x in (GLU_P, BR_P, OUT_P, UP_P, DOWN_P, GLU_T, BR_T, OUT_T, UP_T, DOWN_T))

PRODUCTS = (["norm1", "s5_bT"] + ["lev0", "lev1", "hg_vT"] + [f"lev{k}" for k in range(2, LEVELS + 1)]
            + ["hg_o", "hg_ss", "q_ss", "k_ss", "sb_vT", "z0", "z1", "within0", "within1", "sb_o"]
            + ["bu0", "bu1", "bu2", "s5_y0", "bu3", "bu4", "s5_y1", "bu5", "bu6", "s5_y2", "bu7", "s5_y3", "norm2"])
M = {name: m for m, name in enumerate(PRODUCTS)}

AT = {"norm1": 6, "s5_bT": 9, "hg_vT": 14, "hg_o": 29, "hg_ss": 30, "q_ss": 34, "k_ss": 34, "sb_vT": 35,
      "z0": 38, "z1": 38, "within0": 41, "within1": 41, "sb_o": 44}
AT.update({f"lev{k}": 11 + 2 * k for k in range(LEVELS + 1)})
AT.update({f"bu{k}": 47 + 3 * k for k in range(8)})
AT.update({f"s5_y{c}": 54 + 6 * c for c in range(4)})
TABLE_AT = [42, 47, 54, 60]

HEAD_ORDER = [("x", 0), ("w", 0), ("x", 1), ("w", 1), ("x", 2), ("x", 3), ("w", 2), ("w", 3)]

MAGIC = 12582912.0
LN2 = math.log(2.0)
LN2_HI = 0.693359375
COARSE = 3072.0
TWO_PI = 6.283185307179586
TWO_PI_HI = 6.28125
BELOW_PI = 3.1415925


def layer(nc, xT, w_in, w_glu, w_br, w_out, w_up, w_down, norm_mix, norm_ffn, hg_gain, s5_small, s5_b, s5_c,
          s5_skip, sb_gain, conv, out):
    ctx = ExitStack()
    with ctx:
        def sb(name, shape, dt=F32, scope=None):
            return (scope or ctx).enter_context(nc.sbuf_tensor(name, shape, dt))

        raw = [sb(f"raw{s}", [P, PIECE * P]) for s in range(RING)]
        w_hi = [sb(f"w_hi{s}", [P, PIECE * P], F32R) for s in range(RING)]
        w_lo = [sb(f"w_lo{s}", [P, PIECE * P], F32R) for s in range(RING)]
        half = [sb(f"half{s}", [P, SEQ]) for s in range(2)]
        ones = sb("ones", [P, P])
        eye = sb("eye", [P, P])
        upper = sb("upper", [P, P])
        lower = sb("lower", [P, P])
        level_mask = sb("level_mask", [P, LEVELS, P], U8)
        gain_mix = sb("gain_mix", [P, KT])
        gain_ffn = sb("gain_ffn", [P, KT])
        gain_hg = sb("gain_hg", [P, HEADS])
        gain_sb = sb("gain_sb", [P, 2])
        skip_s5 = sb("skip_s5", [P, CT])
        half_pi = sb("half_pi", [P, 1])
        taps = sb("taps", [P, UP_TILES, 3])
        rstd = sb("rstd", [P, SEQ])
        var = sb("var", [P, SEQ])
        root = sb("root", [P, SEQ])

        late = ExitStack()
        act = sb("act", [P, FT, 2, SEQ], F32R, late)
        x1 = sb("x1", [P, KT, SEQ], F32, late)
        h2 = sb("h2", [P, KT, 2, SEQ], F32R, late)
        sum_u = sb("sum_u", [P, 2, SEQ], F32, late)
        padded = sb("padded", [P, 2, SEQ + 2], F32, late)
        convd = sb("convd", [P, 4, SEQ], F32, late)
        silu = sb("silu", [P, SEQ], F32, late)
        late.close()

        early = ExitStack()
        a_in = sb("a_in", [P, KT, 2, SEQ], F32R, early)
        gates = sb("gates", [P, N_BRANCH * KT, SEQ], F32, early)
        s5_in = sb("s5_in", [P, 3, ST], F32, early)
        s5_t = sb("s5_t", [P, 13, ST], F32, early)
        s5_bT = sb("s5_bT", [P, 2, CT, P], F32, early)
        s5_cT = sb("s5_cT", [P, 2, ST, 2, S5_CH], F32, early)
        time_f = sb("time_f", [P, SEQ], F32, early)
        proj0 = sb("proj0", [P, 5, CT, SEQ], F32, early)
        mixing = ExitStack()
        proj1 = sb("proj1", [P, 3, CT, SEQ], F32, mixing)
        tmp = sb("tmp", [P, 7, 1024], F32, mixing)
        mixing.close()
        splits = ExitStack()
        glu_in = sb("glu_in", [P, CT, 2, SEQ], F32R, splits)
        o_sb = sb("o_sb", [P, CT, 2, SEQ], F32R, splits)
        o_hg = sb("o_hg", [P, CT, 2, SEQ], F32R, splits)
        o_s5 = sb("o_s5", [P, CT, 2, SEQ], F32R, splits)
        gated = sb("gated", [P, 6, SEQ], F32, splits)
        merged = sb("merged", [P, 2, SEQ], F32, splits)
        splits.close()
        early.close()
        x_first = gates[:, 0:KT, :]
        squares = gates[:, KT:2 * KT, :]

        def group(g):
            return proj0[:, g, :, :] if g < 5 else proj1[:, g - 5, :, :]

        def proj(n):
            return group(n // CT)[:, n % CT, :] if n < 8 * CT else gates[:, n - 8 * CT, :]

        def flat(x):
            return x.rearrange("p a b -> p (a b)")

        T = [tmp[:, i, :] for i in range(7)]
        T4 = [t.rearrange("p (c t) -> p c t", c=4) for t in T]
        T2 = [tmp[:, i, :].rearrange("p (s t) -> p s t", t=P) for i in range(7)]

        bank = [ctx.enter_context(nc.psum_tensor(f"bank{b}", [P, 512], F32)) for b in range(BANKS)]
        pair = [ctx.enter_context(nc.psum_tensor(f"pair{b}", [P, 1024], F32)) for b in range(2)]

        def product(name):
            return pair[M[name] % 2]

        sems = {}

        def S(name):
            if name not in sems:
                sems[name] = ctx.enter_context(nc.semaphore(name))
            return sems[name]

        raw_landed = [S(f"raw_landed{s}") for s in range(RING)]
        hi_ready, lo_ready, piece_used = S("hi_ready"), S("lo_ready"), S("piece_used")
        half_copied, tile_summed, tile_scaled = S("half_copied"), S("tile_summed"), S("tile_scaled")
        product_done = S("product_done")
        pair_taken = [S("pair_taken0"), S("pair_taken1")]

        counts = {}

        def link(eng, ins, name):
            counts[name] = counts.get(name, 0) + 1
            ins.then_inc(S(name), 1)
            eng.wait_ge(S(name), counts[name])

        def wait_product(eng, name):
            eng.wait_ge(product_done, M[name] + 1)

        def taken(ins, name):
            return ins.then_inc(pair_taken[M[name] % 2], 1)

        def wait_taken(eng, name):
            eng.wait_ge(pair_taken[M[name] % 2], M[name] // 2 + 1)

        block = ctx.enter_context(nc.Block())

        @block.sync
        def _(sp):
            def load(p, c, src, width=PIECE * P):
                if not (isinstance(p, int) and p < RING):
                    sp.wait_ge(lo_ready, p - (RING - 1))
                sp.dma_start(raw[c % RING][:, 0:width], src).then_inc(raw_landed[c % RING], 16)

            for kind, q in HEAD_ORDER:
                if kind == "x":
                    sp.dma_start(x_first[:, 4 * q:4 * q + 4, :], xT[:, 4 * q:4 * q + 4, :]).then_inc(S(f"x_landed{q}"), 16)
                else:
                    load(q, q, w_in[q])
            with sp.Fori(1, GLU_P // RING) as i:
                for c in range(RING):
                    load(i * RING + c, c, w_in[i * RING + c])
            for c in range(CT):
                load(GLU_P + c, c, w_glu[c])
            with sp.Fori(0, KT // 2) as i:
                for c in range(RING):
                    blocks = PIECE if c % 2 == 0 else N_BRANCH * CT - PIECE
                    load(i * RING + (BR_P + c), c, w_br[i * 2 + c // 2, :, (c % 2) * PIECE * P:(c % 2 * PIECE + blocks) * P],
                         blocks * P)
            with sp.Fori(0, 2 * OUT_TILES // RING) as i:
                for c in range(RING):
                    load(i * RING + (OUT_P + c), c, w_out[i * RING + c])
            with sp.Fori(0, 2 * UP_TILES // RING) as i:
                for c in range(RING):
                    load(i * RING + (UP_P + c), c, w_up[i * RING + c])
            with sp.Fori(0, DOWN_TILES // 2) as i:
                c = 0
                for t in range(2):
                    at = 0
                    for blocks in DOWN_PIECES:
                        load(i * (2 * len(DOWN_PIECES)) + (DOWN_P + c), c, w_down[i * 2 + t, :, at * P:(at + blocks) * P], blocks * P)
                        at += blocks
                        c += 1
            last = DOWN_TILES // BANKS - 1
            for j in range(BANKS):
                sp.wait_ge(S("y_ready"), last * BANKS + j + 1)
                sp.dma_start(out[last, :, j:j + 1, :], x1[:, last * BANKS + j:last * BANKS + j + 1, :]).then_inc(S("stored_last"), 16)
            sp.wait_ge(S("stored_last"), 16 * BANKS)

        @block.tensor
        def _(pe):
            def piece(b, p, c, blocks, rhs, first, last):
                if p is not None:
                    pe.wait_ge(lo_ready, p + 1)
                w, l = w_hi[c % RING], w_lo[c % RING]
                for n, k in enumerate(blocks):
                    a = rhs(n)
                    pe.matmul(bank[b][:, :], w[:, k * P:(k + 1) * P], a.rearrange("p a t -> p (a t)"),
                              start=first and n == 0, stop=False, skip_group_check=True)
                    mm = pe.matmul(bank[b][:, 0:SEQ], l[:, k * P:(k + 1) * P], a[:, 0, :],
                                   start=False, stop=last and n == len(blocks) - 1, skip_group_check=True)
                return mm

            def bank_free(n):
                if not (isinstance(n, int) and n < BANKS):
                    pe.wait_ge(tile_summed, n - (BANKS - 1))

            def start_product(name):
                m = M[name]
                if m >= 2:
                    pe.wait_ge(pair_taken[m % 2], m // 2)
                return product(name)

            def fp32_product(name, ops):
                out_ = start_product(name)
                for (p0, p1, c0, c1), lhsT, rhs, start, stop in ops:
                    mm = pe.matmul(out_[p0:p1, c0:c1], lhsT, rhs, start=start, stop=stop, skip_group_check=True)
                mm.then_inc(product_done, 1)

            def transposes(name, blocks):
                out_ = start_product(name)
                for i, b in enumerate(blocks):
                    mm = pe.transpose(out_[:, i * P:(i + 1) * P], b, eye[:, :])
                mm.then_inc(product_done, 1)

            def level(k):
                if k == 0:
                    pe.wait_ge(S("hg_k"), 1)
                    pe.wait_ge(tile_scaled, CT * (HG_Q + 1))
                    ops = [((0, P, (4 * b + h) * P, (4 * b + h + 1) * P), T4[2][:, h, b * P:(b + 1) * P],
                            group(HG_Q)[:, h, b * P:(b + 1) * P], True, True) for b in range(2) for h in range(HEADS)]
                else:
                    pe.wait_ge(S("hg_factors"), 2 * k)
                    W = T4[4 + k % 2]
                    if k < LEVELS:
                        ops = [((0, P, (4 * b + h) * P, (4 * b + h + 1) * P), W[:, h, b * P:(b + 1) * P],
                                W[:, h, b * P:(b + 1) * P], True, True) for b in range(2) for h in range(HEADS)]
                    else:
                        ops = [((0, P, h * P, (h + 1) * P), W[:, h, 0:P], W[:, h, P:SEQ], True, True) for h in range(HEADS)]
                fp32_product(f"lev{k}", ops)

            def mixers(n):
                if n == AT["norm1"]:
                    pe.wait_ge(S("x_sq_sum"), 4)
                    fp32_product("norm1", [((0, P, 0, SEQ), ones[:, :], squares[:, 0, :], True, True)])
                if n == AT["s5_bT"]:
                    pe.wait_ge(S("s5_bb"), 4)
                    transposes("s5_bT", [T[1][:, (4 * r + c) * P:(4 * r + c + 1) * P] for r in range(2) for c in range(CT)])
                for k in range(LEVELS + 1):
                    if n == AT[f"lev{k}"]:
                        level(k)
                if n == AT["hg_vT"]:
                    pe.wait_ge(tile_scaled, CT * (HG_I + 1))
                    transposes("hg_vT", [group(HG_I)[:, h, b * P:(b + 1) * P] for b in range(2) for h in range(HEADS)])
                if n == AT["hg_o"]:
                    for name in ("hg_vT", "lev7", "lev8"):
                        wait_taken(pe, name)
                    v = group(HG_F).rearrange("p c (b t) -> p (c b) t", b=2)
                    ops = []
                    for h in range(HEADS):
                        ops += [((0, P, h * SEQ, h * SEQ + P), v[:, h, :], T2[6][:, h, :], True, True),
                                ((0, P, h * SEQ + P, (h + 1) * SEQ), v[:, h, :], T2[0][:, h, :], True, False),
                                ((0, P, h * SEQ + P, (h + 1) * SEQ), v[:, 4 + h, :], T2[6][:, 4 + h, :], False, True)]
                    fp32_product("hg_o", ops)
                for name, sem, src in (("hg_ss", None, T[1]), ("q_ss", "q_sq", T[0]), ("k_ss", "k_sq", T[1])):
                    if n == AT[name]:
                        if sem:
                            pe.wait_ge(S(sem), 1)
                        else:
                            wait_taken(pe, "hg_o")
                        fp32_product(name, [((0, P, c * 512, (c + 1) * 512), ones[:, :], src[:, c * 512:(c + 1) * 512], True, True)
                                            for c in range(2)])
                if n == AT["sb_vT"]:
                    pe.wait_ge(tile_scaled, CT * (SB_V + 1))
                    transposes("sb_vT", [group(SB_V)[:, h, b * P:(b + 1) * P] for b in range(2) for h in range(HEADS)])
                for hh in range(2):
                    if n == AT[f"z{hh}"]:
                        pe.wait_ge(S("q_normed"), 1)
                        pe.wait_ge(S("k_normed"), 1)
                        q, k = group(SB_Q), group(SB_K)
                        fp32_product(f"z{hh}", [((0, P, i * SEQ, (i + 1) * SEQ), k[:, 2 * hh + i, 0:P], q[:, 2 * hh + i, :], True, True)
                                                for i in range(2)]
                                     + [((0, P, 512 + i * P, 512 + (i + 1) * P), k[:, 2 * hh + i, P:SEQ], q[:, 2 * hh + i, P:SEQ], True, True)
                                        for i in range(2)])
                    if n == AT[f"within{hh}"]:
                        pe.wait_ge(S("sb_masked"), 2 * (hh + 1))
                        sp_ = tmp[:, 4:6, :].rearrange("p a b -> p (a b)")[:, 768 * hh:768 * (hh + 1)]
                        ops = []
                        for i in range(2):
                            ops += [((0, P, i * SEQ, (i + 1) * SEQ), lower[:, :], sp_[:, i * SEQ:(i + 1) * SEQ], True, False),
                                    ((0, P, i * SEQ + P, (i + 1) * SEQ), ones[:, :], sp_[:, 512 + i * P:512 + (i + 1) * P], False, True)]
                        for i in range(2):
                            ops += [((0, P, 512 + i * P, 512 + (i + 1) * P), lower[:, :], sp_[:, 512 + i * P:512 + (i + 1) * P], True, True)]
                        fp32_product(f"within{hh}", ops)
                if n == AT["sb_o"]:
                    pe.wait_ge(S("sb_w"), 4)
                    wait_taken(pe, "sb_vT")
                    v = group(HG_Q).rearrange("p c (b t) -> p (c b) t", b=2)
                    w = tmp[:, 0:2, :].rearrange("p a b -> p (a b)")
                    ops = []
                    for h in range(HEADS):
                        at = 768 * (h // 2)
                        i = h % 2
                        ops += [((0, P, h * SEQ, (h + 1) * SEQ), v[:, h, :], w[:, at + i * SEQ:at + (i + 1) * SEQ], True, False),
                                ((0, P, h * SEQ + P, (h + 1) * SEQ), v[:, 4 + h, :], w[:, at + 512 + i * P:at + 512 + (i + 1) * P], False, True)]
                    fp32_product("sb_o", ops)
                for k in range(8):
                    if n == AT[f"bu{k}"]:
                        if k == 0:
                            wait_taken(pe, "s5_bT")
                            pe.wait_ge(tile_scaled, CT * (S5_U + 1))
                        ops = []
                        for i in range(2):
                            for r in range(2):
                                s = 2 * k + i
                                rows = slice(32 * (s % 4), 32 * (s % 4) + 32)
                                ops.append(((0, P, (2 * i + r) * SEQ, (2 * i + r + 1) * SEQ), s5_bT[rows, r, s // 4, :],
                                            group(S5_U)[rows, s // 4, :], True, True))
                        fp32_product(f"bu{k}", ops)
                for c in range(CT):
                    if n == AT[f"s5_y{c}"]:
                        pe.wait_ge(S("s5_x"), 4 * (c + 1))
                        ops = [((32 * i, 32 * i + 32, 0, SEQ), s5_cT[:, r, 4 * c + i, :, :].rearrange("p a b -> p (a b)"),
                                proj1[:, r, i, :], r == 0, r == 1) for r in range(2) for i in range(4)]
                        fp32_product(f"s5_y{c}", ops)

            def a_in_block(n, k):
                if n == 0:
                    pe.wait_ge(S("a_in_lo"), k + 1)
                return a_in[:, k, :, :]

            for n in range(IN_TILES):
                bank_free(n)
                for h in range(2):
                    mm = piece(n % BANKS, 2 * n + h, 2 * n + h, range(PIECE), lambda k: a_in_block(n, PIECE * h + k), h == 0, h == 1)
                    mm.then_inc(piece_used, 1)
                mixers(n)

            pe.wait_ge(S("glu_in_lo"), 1)
            for m in range(CT):
                for i in range(2):
                    n = GLU_T + 2 * m + i
                    bank_free(n)
                    mm = piece(n % BANKS, GLU_P + m if i == 0 else None, GLU_P + m, range(CT * i, CT * (i + 1)),
                               lambda k: glu_in[:, k, :, :], True, True)
                    mm.then_inc(piece_used if i else S("glu_first"), 1)

            pe.wait_ge(S("o_split"), 2)

            def branch_tile(i, j):
                t = 3 * j
                for b, (c, lo, src) in enumerate(((0, 0, o_hg), (0, CT, o_sb), (1, 0, o_s5))):
                    n = i * (3 * RING) + (BR_T + t + b)
                    bank_free(n)
                    if b == 2:
                        pe.wait_ge(S("o_s5_lo"), CT)
                    mm = piece((t + b) % BANKS, i * (2 * RING) + (BR_P + 2 * j + c) if b != 1 else None, 2 * j + c,
                               range(lo, lo + CT), lambda k: src[:, k, :, :], True, True)
                    mm.then_inc(S("br_first") if b == 0 else piece_used, 1)

            with pe.Fori(0, KT // RING) as i:
                for j in range(RING):
                    branch_tile(i, j)

            def after(sem, j, k, src):
                if j == 0:
                    pe.wait_ge(S(sem), k + 1)
                return src[:, k, :, :]

            with pe.Fori(0, OUT_TILES // BANKS) as i:
                for j in range(BANKS):
                    bank_free(i * BANKS + (OUT_T + j))
                    for h in range(2):
                        mm = piece(j, i * (2 * BANKS) + (OUT_P + 2 * j + h), 2 * j + h, range(PIECE),
                                   lambda k: after("merged_lo", j, PIECE * h + k, a_in), h == 0, h == 1)
                        mm.then_inc(piece_used, 1)

            def up_body(i):
                for j in range(BANKS):
                    bank_free(i * BANKS + (UP_T + j))
                    for h in range(2):
                        mm = piece(j, i * (2 * BANKS) + (UP_P + 2 * j + h), 2 * j + h, range(PIECE),
                                   lambda k: after("h2_lo", j if isinstance(i, int) else 1, PIECE * h + k, h2), h == 0, h == 1)
                        mm.then_inc(piece_used, 1)
                    if isinstance(i, int) and j == 0:
                        pe.wait_ge(S("x1_sq_sum"), KT)
                        fp32_product("norm2", [((0, P, 0, SEQ), ones[:, :], root[:, :], True, True)])

            up_body(0)
            with pe.Fori(1, UP_TILES // BANKS) as i:
                up_body(i)

            with pe.Fori(0, DOWN_TILES // BANKS) as i:
                c = 0
                for j in range(BANKS):
                    bank_free(i * BANKS + (DOWN_T + j))
                    at = 0
                    for blocks in DOWN_PIECES:
                        if j == 0:
                            pe.wait_ge(S("act_lo"), at + blocks)
                        mm = piece(j, i * (BANKS * len(DOWN_PIECES)) + (DOWN_P + c), c, range(blocks),
                                   lambda k: act[:, at + k, :, :], at == 0, at + blocks == FT)
                        mm.then_inc(piece_used, 1)
                        at += blocks
                        c += 1

        HG_FF, HG_QQ, HG_II, HG_GG, UU, SQ, SK = (group(g) for g in (HG_F, HG_Q, HG_I, HG_G, S5_U, SB_Q, SB_K))
        Z = tmp[:, 0:2, :].rearrange("p a b -> p (a b)")[:, 0:1536]
        LOG1P = tmp[:, 2:4, :].rearrange("p a b -> p (a b)")[:, 0:1536]
        SOFTP = tmp[:, 4:6, :].rearrange("p a b -> p (a b)")[:, 0:1536]

        def halves(x, h):
            v = x.rearrange("p c (n r t) -> p (c n) r t", r=2, t=h)
            return v[:, :, 0, :], v[:, :, 1, :]

        def bc(x, shape):
            return x.broadcast_to(shape)

        def s5_tables(g):
            return (T4[2], T4[3]) if g % 2 == 0 else (T4[0], T4[1])

        def s5_slice(k):
            return slice(2 * (k % 2), 2 * (k % 2) + 2)

        SIDX = {n: i for i, n in enumerate(("dt", "mag", "theta", "turns", "turns_lo", "r", "cos", "sin", "t1", "t2", "t3", "zr", "zi"))}

        def s5v(name):
            return s5_t[:, SIDX[name], :]

        @block.scalar
        def _(act_e):
            def hi(i, per, p0, blocks=PIECE):
                p, s = i * per + p0, p0 % RING
                act_e.wait_ge(raw_landed[s], i * (16 * per // RING) + 16 * (p0 // RING + 1))
                if not (isinstance(p, int) and p < RING):
                    act_e.wait_ge(piece_used, p - (RING - 1))
                act_e.activation(w_hi[s][:, 0:blocks * P], raw[s][:, 0:blocks * P], ACT.Copy).then_inc(hi_ready, 1)

            def copy_half(n, j, done, value):
                act_e.wait_ge(done, value)
                if not (isinstance(n, int) and n < 2):
                    act_e.wait_ge(tile_summed, n - 1)
                act_e.activation(half[j % 2][:, :], bank[j % BANKS][:, SEQ:2 * SEQ], ACT.Copy).then_inc(half_copied, 1)

            def run(name, out_, in_, func, **kw):
                link(act_e, act_e.activation(out_, in_, func, **kw), name)

            def rough_root(name, y, v):
                act_e.wait_ge(S(name + "_var"), 1)
                run(name + "_root", y, v, ACT.Ln)
                run(name + "_root", y, y, ACT.Exp, scale=-0.5)

            def sigmoid_gates(b):
                act_e.wait_ge(tile_scaled, 8 * CT + 4 * (b + 1))
                g = flat(gates[:, 4 * b:4 * b + 4, :])
                act_e.activation(g, g, ACT.Sigmoid).then_inc(S("gate_ready"), 1)

            def mixers(n):
                if n == 4:
                    act_e.wait_ge(S("s5_r"), 1)
                    run("s5_sin", s5v("sin"), s5v("r"), ACT.Sin)
                    run("s5_absr", s5v("t2"), s5v("r"), ACT.Abs)
                    run("s5_cos", s5v("cos"), s5v("t2"), ACT.Sin, scale=-1.0, bias=half_pi[:, 0:1])
                    c_im = s5_cT[:, 1, :, :, :].rearrange("p s a c -> p (s a c)")
                    run("s5_cT_signed", c_im, c_im, ACT.Copy, scale=-1.0)
                if n == AT["norm1"] + 1:
                    rough_root("norm1", root[:, :], var[:, :])
                if n == AT["s5_bT"] + 1:
                    wait_product(act_e, "s5_bT")
                    taken(act_e.activation(s5_bT[:, :, :, :].rearrange("p r c s -> p (r c s)"), product("s5_bT")[:, :], ACT.Copy), "s5_bT")
                if n == 9:
                    act_e.wait_ge(S("s5_bb"), 4)
                    act_e.wait_ge(tile_scaled, CT * (HG_F + 1))
                    f = flat(HG_FF)
                    run("hg_abs", T[0], f, ACT.Abs)
                    run("hg_exp", T[0], T[0], ACT.Exp, scale=-1.0)
                    run("hg_ln", T[0], T[0], ACT.Ln, bias=1.0)
                if n == 11:
                    act_e.wait_ge(S("hg_sp"), 1)
                    run("hg_k", T[2], T[2], ACT.Exp, scale=-1.0)
                for k in range(1, LEVELS + 1):
                    if n == AT[f"lev{k}"]:
                        if k == 1:
                            act_e.wait_ge(S("hg_lf"), 1)
                            act_e.wait_ge(S("hg_ex0"), 1)
                        else:
                            act_e.wait_ge(S("hg_segments"), 2 * (k - 1))
                        if k > 2:
                            wait_product(act_e, f"lev{k - 2}")
                        W = halves(T4[4 + k % 2], 2 ** (k - 1))
                        act_e.activation(W[1], halves(T4[1], 2 ** (k - 1))[1], ACT.Exp).then_inc(S("hg_decay"), 1)
                        act_e.activation(W[0], halves(T4[3], 2 ** (k - 1))[0], ACT.Exp).then_inc(S("hg_decay"), 1)
                if n == AT["hg_vT"] + 1:
                    wait_product(act_e, "hg_vT")
                    taken(act_e.activation(flat(HG_FF), product("hg_vT")[:, :], ACT.Copy), "hg_vT")
                if n == AT["hg_o"] + 1:
                    wait_product(act_e, "hg_o")
                    run("hg_o_out", flat(HG_II), product("hg_o")[:, :], ACT.Copy)
                    taken(act_e.activation(T[1], product("hg_o")[:, :], ACT.Square), "hg_o")
                    act_e.wait_ge(tile_scaled, CT * (HG_G + 1))
                    run("hg_sig", T[5], flat(HG_GG), ACT.Sigmoid)
                if n == AT["hg_ss"] + 1:
                    rough_root("hg", T[3], T[2])
                if n == AT["q_ss"]:
                    act_e.wait_ge(tile_scaled, CT * (SB_K + 1))
                    wait_product(act_e, "hg_ss")
                    run("q_sq", T[0], flat(SQ), ACT.Square)
                    run("k_sq", T[1], flat(SK), ACT.Square)
                if n == AT["q_ss"] + 1:
                    rough_root("q", T[3], T[2])
                if n == AT["sb_vT"] + 1:
                    rough_root("k", T[6], T[5])
                    wait_product(act_e, "sb_vT")
                    taken(act_e.activation(flat(HG_QQ), product("sb_vT")[:, :], ACT.Copy), "sb_vT")
                if n == AT["z0"] + 1:
                    for hh in range(2):
                        wait_product(act_e, f"z{hh}")
                        taken(act_e.activation(Z[:, 768 * hh:768 * (hh + 1)], product(f"z{hh}")[:, 0:768], ACT.Copy), f"z{hh}")
                    for hh in range(2):
                        wait_taken(act_e, f"z{hh}")
                    run("sb_abs", LOG1P, Z, ACT.Abs)
                    run("sb_exp", LOG1P, LOG1P, ACT.Exp, scale=-1.0)
                    run("sb_ln", LOG1P, LOG1P, ACT.Ln, bias=1.0)
                if n == AT["within0"] + 1:
                    for hh in range(2):
                        wait_taken(act_e, f"within{hh}")
                    run("sb_wexp", Z, Z, ACT.Exp)
                if n == AT["sb_o"] + 1:
                    wait_product(act_e, "sb_o")
                    taken(act_e.activation(flat(HG_II), product("sb_o")[:, :], ACT.Copy), "sb_o")
                for g in range(4):
                    if n == TABLE_AT[g] + 3:
                        act_e.wait_ge(S("s5_phase2"), 6 * (g + 1))
                        cos, sin = s5_tables(g)
                        run("s5_table", flat(sin), flat(cos), ACT.Sin, scale=6.283185)
                        run("s5_table", flat(cos), flat(cos), ACT.Abs)
                        run("s5_table", flat(cos), flat(cos), ACT.Sin, scale=-6.283185, bias=half_pi[:, 0:1])
                if n == 74:
                    act_e.wait_ge(S("s5_y"), CT)
                    act_e.wait_ge(S("s5_x"), 16)
                    run("gelu_sq", T[4], flat(UU), ACT.Square)
                if n == 75:
                    act_e.wait_ge(S("gelu_arg"), 2)
                    run("gelu_sig", T[4], T[4], ACT.Sigmoid, scale=1.5957691216057308)
                if n == 76:
                    act_e.wait_ge(S("gelu"), 1)
                    wait_product(act_e, "s5_y3")
                    run("glu_in_hi", glu_in[:, :, 0, :], UU, ACT.Copy)
                if n == 78:
                    act_e.wait_ge(S("hg_out"), HEADS)
                    run("o_hi", o_hg[:, :, 0, :], HG_GG, ACT.Copy)
                    wait_taken(act_e, "sb_o")
                    run("o_hi", o_sb[:, :, 0, :], HG_II, ACT.Copy)
                for b in range(11):
                    if n == 4 * b + 40:
                        sigmoid_gates(b)

            act_e.dma_start(gain_mix[:, :], norm_mix).then_inc(S("gains_landed"), 16)
            act_e.wait_ge(S("gains_landed"), 16)
            for kind, k in HEAD_ORDER:
                if kind == "w":
                    hi(0, RING, k)
                    continue
                act_e.wait_ge(S(f"x_landed{k}"), 16)
                for c in range(4 * k, 4 * k + 4):
                    act_e.activation(a_in[:, c, 0, :], x_first[:, c, :], ACT.Copy, scale=gain_mix[:, c:c + 1]).then_inc(S("a_in_hi"), 1)
            for q in range(4):
                act_e.activation(squares[:, 4 * q:4 * q + 4, :], x_first[:, 4 * q:4 * q + 4, :], ACT.Square).then_inc(S("x_sq"), 1)

            for n in range(IN_TILES):
                for p in (2 * n + 4, 2 * n + 5):
                    hi(0, RING, p)
                copy_half(n, n, piece_used, 2 * n + 2)
                mixers(n + 1)

            def glu_gate(m):
                act_e.wait_ge(tile_summed, GLU_T + 2 * m + 2)
                act_e.activation(HG_QQ[:, m, :], HG_QQ[:, m, :], ACT.Sigmoid).then_inc(S("glu_sig"), 1)

            def glu_split(m):
                act_e.wait_ge(S("glu_out"), m + 1)
                act_e.activation(o_s5[:, m, 0, :], HG_FF[:, m, :], ACT.Copy).then_inc(S("o_s5_hi"), 1)

            sigmoid_gates(11)
            for m in range(CT):
                copy_half(GLU_T + 2 * m, 2 * m, S("glu_first"), m + 1)
                copy_half(GLU_T + 2 * m + 1, 2 * m + 1, piece_used, GLU_P + m + 1)
                hi(0, RING, BR_P + m, PIECE if m % 2 == 0 else CT)
                glu_gate(m)
                if m:
                    glu_split(m - 1)
            glu_split(CT - 1)

            def merged_hi(u, j):
                act_e.wait_ge(S("merged"), u + 1)
                act_e.activation(a_in[:, u, 0, :], merged[:, j % 2, :], ACT.Copy).then_inc(S("merged_hi"), 1)

            def branches(i, last):
                for j in range(RING):
                    for b in range(3):
                        if b:
                            if last and j >= 2:
                                hi(0, RING, OUT_P + 2 * (j - 2) + b - 1)
                            else:
                                hi(i, 2 * RING, BR_P + 2 * (j + 2) + b - 1, PIECE if b == 1 else CT)
                        n = i * (3 * RING) + (BR_T + 3 * j + b)
                        done, value = ((S("br_first"), i * RING + (j + 1)) if b == 0 else
                                       (piece_used, i * (2 * RING) + (BR_P + 2 * j + b)))
                        copy_half(n, 3 * j + b, done, value)
                    if not (isinstance(i, int) and i == 0 and j == 0):
                        merged_hi(i * RING + (j - 1), j - 1)

            branches(0, False)
            with act_e.Fori(1, KT // RING - 1) as i:
                branches(i, False)
            branches(KT // RING - 1, True)
            merged_hi(KT - 1, KT - 1)

            def outs(i, last):
                for j in range(BANKS):
                    for c in range(2):
                        if last and j >= 2:
                            hi(0, RING, UP_P + 2 * (j - 2) + c)
                        else:
                            hi(i, 2 * BANKS, OUT_P + 2 * (j + 2) + c)
                    copy_half(i * BANKS + (OUT_T + j), j, piece_used, i * (2 * BANKS) + (OUT_P + 2 * j + 2))
                    act_e.wait_ge(S("x1_ready"), i * BANKS + (j + 1))
                    t = i * BANKS + j
                    act_e.activation(h2[:, t, 0, :], x1[:, t, :], ACT.Copy, scale=gain_ffn[:, bass.ds(t, 1)]).then_inc(S("h2_hi"), 1)

            with act_e.Fori(0, OUT_TILES // BANKS - 1) as i:
                outs(i, False)
            outs(OUT_TILES // BANKS - 1, True)

            def ups(i, last):
                for j in range(BANKS):
                    first = isinstance(i, int) and i == 0
                    t = i * BANKS + j
                    if j % 2 == 1 and not (first and j < 3):
                        q = i * 2 + (j - 3) // 2
                        act_e.wait_ge(S("conv_done"), t - 1)
                        act_e.activation(silu[:, :], convd[:, (j - 3) % 4, :], ACT.Silu).then_inc(S("silu_done"), 1)
                    for c in range(2):
                        if last and j >= 2:
                            hi(0, RING, DOWN_P + 2 * (j - 2) + c)
                        else:
                            hi(i, 2 * BANKS, UP_P + 2 * (j + 2) + c)
                    if first and j == 1:
                        rough_root("norm2", root[:, :], var[:, :])
                    copy_half(i * BANKS + (UP_T + j), j, piece_used, i * (2 * BANKS) + (UP_P + 2 * j + 2))
                    if not (first and j == 0):
                        tap2_at(i, j - 1)
                    if j % 2 == 1 and not (first and j < 3):
                        hidden_hi(q, j)

            def tap2_at(i, j):
                t = i * BANKS + j
                act_e.wait_ge(S("up_scaled"), t + 1)
                if not (isinstance(i, int) and t < 4):
                    act_e.wait_ge(S("act_lo"), i * 2 + (j // 2 - 1))
                act_e.activation(convd[:, j % 4, :], padded[:, j % 2, 2:], ACT.Copy, scale=taps[:, t, 2:3]).then_inc(S("tap2"), 1)

            def hidden_hi(q, j):
                act_e.wait_ge(S("hidden"), q + 1)
                act_e.activation(act[:, q, 0, :], convd[:, (j - 2) % 4, :], ACT.Copy).then_inc(S("act_hi"), 1)

            ups(0, False)
            with act_e.Fori(1, UP_TILES // BANKS - 1) as i:
                ups(i, False)
            ups(UP_TILES // BANKS - 1, True)
            tap2_at(UP_TILES // BANKS, -1)
            act_e.wait_ge(S("conv_done"), UP_TILES)
            act_e.activation(silu[:, :], convd[:, 2, :], ACT.Silu).then_inc(S("silu_done"), 1)
            hidden_hi(FT - 1, 1)

            def downs(i, last):
                n_p = len(DOWN_PIECES)
                for j in range(BANKS):
                    for c in range(n_p):
                        p = j * n_p + RING + c
                        if not last or p < BANKS * n_p:
                            hi(i, BANKS * n_p, DOWN_P + p, DOWN_PIECES[p % n_p])
                    copy_half(i * BANKS + (DOWN_T + j), j, piece_used, i * (BANKS * n_p) + (DOWN_P + n_p * (j + 1)))

            with act_e.Fori(0, DOWN_TILES // BANKS - 1) as i:
                downs(i, False)
            downs(DOWN_TILES // BANKS - 1, True)

        @block.vector
        def _(ve):
            def lo(i, per, p0, blocks=PIECE):
                p, s = i * per + p0, p0 % RING
                ve.wait_ge(hi_ready, p + 1)
                w = slice(0, blocks * P)
                ve.tensor_tensor(w_lo[s][:, w], raw[s][:, w], w_hi[s][:, w].bitcast(F32), ALU.subtract).then_inc(lo_ready, 1)

            def add_halves(n, j, dest):
                ve.wait_ge(half_copied, n + 1)
                ve.tensor_tensor(dest, bank[j % BANKS][:, 0:SEQ], half[j % 2][:, :], ALU.add).then_inc(tile_summed, 1)

            def tt(name, out_, a, b, op):
                link(ve, ve.tensor_tensor(out_, a, b, op), name)

            def ts(name, out_, a, s1, s2, op0, op1=None):
                ins = ve.tensor_scalar(out_, a, s1, None, op0) if op1 is None else ve.tensor_scalar(out_, a, s1, s2, op0, op1)
                link(ve, ins, name)

            def stt(name, out_, a, s_, b, op0, op1):
                link(ve, ve.scalar_tensor_tensor(out_, a, s_, b, op0, op1), name)

            def inverse_root(name, v, y, t):
                ve.wait_ge(S(name + "_root"), 2)
                tt(name + "_newton", t, y, y, ALU.mult)
                stt(name + "_newton", t, t, -0.5, v, ALU.mult, ALU.mult)
                stt(name + "_rstd", y, t, 1.5, y, ALU.add, ALU.mult)

            def token_norm(name):
                ve.wait_ge(S(name + "_root"), 2)
                tt(name + "_newton", rstd[:, :], root[:, :], root[:, :], ALU.mult)
                stt(name + "_newton", rstd[:, :], rstd[:, :], -0.5, var[:, :], ALU.mult, ALU.mult)
                stt(name + "_rstd", rstd[:, :], rstd[:, :], 1.5, root[:, :], ALU.add, ALU.mult)

            def mean(name, out_, of):
                wait_product(ve, name)
                n_feat = D_MODEL if name.startswith("norm") else P
                taken(ve.tensor_scalar(out_, product(name)[:, 0:of], 1.0 / n_feat, EPS, ALU.mult, ALU.add), name)
                wait_taken(ve, name)

            def exact_exp(out_, x):
                c, n_, r, p = "s5_setup", s5v("t1"), s5v("t2"), s5v("t3")
                ts(c, n_, x, 1.0 / LN2, MAGIC, ALU.mult, ALU.add)
                ts(c, n_, n_, MAGIC, None, ALU.subtract)
                stt(c, r, n_, -LN2_HI, x, ALU.mult, ALU.add)
                stt(c, r, n_, -(LN2 - LN2_HI), r, ALU.mult, ALU.add)
                ts(c, p, r, 1.0 / math.factorial(8), None, ALU.mult)
                for d in range(7, 0, -1):
                    stt(c, p, p, 1.0 / math.factorial(d), r, ALU.add, ALU.mult)
                bits = s5v("r").bitcast(I32)
                ts(c, n_, n_, -126.0, 127.0, ALU.max, ALU.min)
                ts(c, bits, n_, 127.0, None, ALU.add)
                ts(c, bits, bits, 23, None, ALU.logical_shift_left)
                stt(c, out_, p, 1.0, s5v("r"), ALU.add, ALU.mult)

            def s5_decay(part):
                if part == 0:
                    ve.wait_ge(S("s5_landed"), 16 * 11)
                    exact_exp(s5v("dt"), s5_in[:, 2, :])
                    tt("s5_setup", s5v("zr"), s5_in[:, 0, :], s5v("dt"), ALU.mult)
                else:
                    exact_exp(s5v("mag"), s5v("zr"))

            def s5_angle():
                c, li = "s5_setup", s5_in[:, 1, :]
                tt(c, s5v("theta"), li, s5v("dt"), ALU.mult)
                ts(c, s5v("t3"), s5v("theta"), 1.0 / TWO_PI, MAGIC, ALU.mult, ALU.add)
                ts(c, s5v("t3"), s5v("t3"), MAGIC, None, ALU.subtract)
                stt(c, s5v("theta"), s5v("t3"), -TWO_PI_HI, s5v("theta"), ALU.mult, ALU.add)
                stt(c, s5v("theta"), s5v("t3"), -(TWO_PI - TWO_PI_HI), s5v("theta"), ALU.mult, ALU.add)
                ts(c, s5v("turns"), s5v("theta"), 1.0 / TWO_PI, None, ALU.mult)
                ts(c, s5v("turns_lo"), s5v("turns"), COARSE, COARSE, ALU.add, ALU.subtract)
                tt(c, s5v("t3"), s5v("turns"), s5v("turns_lo"), ALU.subtract)
                ts(c, s5v("turns"), s5v("turns_lo"), 0.0, None, ALU.add)
                ts(c, s5v("turns_lo"), s5v("t3"), 0.0, None, ALU.add)
                ts("s5_r", s5v("r"), s5v("theta"), BELOW_PI, -BELOW_PI, ALU.min, ALU.max)

            def s5_input_gain():
                c, lr, li = "s5_setup", s5_in[:, 0, :], s5_in[:, 1, :]
                ve.wait_ge(S("s5_cos"), 1)
                tt(c, s5v("cos"), s5v("cos"), s5v("mag"), ALU.mult)
                ts(c, s5v("cos"), s5v("cos"), 1.0, None, ALU.subtract)
                tt(c, s5v("sin"), s5v("sin"), s5v("mag"), ALU.mult)
                tt(c, s5v("t1"), lr, lr, ALU.mult)
                tt(c, s5v("t2"), li, li, ALU.mult)
                tt(c, s5v("t1"), s5v("t1"), s5v("t2"), ALU.add)
                link(ve, ve.reciprocal(s5v("t3"), s5v("t1")), c)
                tt(c, s5v("t1"), s5v("cos"), lr, ALU.mult)
                tt(c, s5v("t2"), s5v("sin"), li, ALU.mult)
                tt(c, s5v("t1"), s5v("t1"), s5v("t2"), ALU.add)
                tt(c, s5v("zr"), s5v("t1"), s5v("t3"), ALU.mult)
                tt(c, s5v("t1"), s5v("sin"), lr, ALU.mult)
                tt(c, s5v("t2"), s5v("cos"), li, ALU.mult)
                tt(c, s5v("t1"), s5v("t1"), s5v("t2"), ALU.subtract)
                tt(c, s5v("zi"), s5v("t1"), s5v("t3"), ALU.mult)

            def s5_input_weights(r):
                c = "s5_setup"
                b = T[0].rearrange("p (r s c) -> p r s c", r=4, c=S5_CH)
                full = [P, ST, S5_CH]
                zr, zi = (bc(s5v(x).unsqueeze(2), full) for x in ("zr", "zi"))
                out_ = T[1].rearrange("p (r s g c) -> p r s g c", r=2, s=ST, g=2)
                tt(c, b[:, 2], b[:, r], zr, ALU.mult)
                tt(c, b[:, 3], b[:, 1 - r], zi, ALU.mult)
                ve.wait_ge(S("s5_zero"), 2)
                for g in range(2):
                    rows = slice(64 * g, 64 * g + 64)
                    tt("s5_bb", out_[rows, r, :, g, :], b[rows, 2], b[rows, 3], ALU.add if r else ALU.subtract)

            def masks(of_levels):
                ve.wait_ge(S("iota"), 3)
                diff, xor = T[4][:, 0:P].bitcast(I32), T[4][:, P:2 * P].bitcast(I32)
                row = T[4][:, 2 * P:3 * P].bitcast(I32)
                if not of_levels:
                    ts("masks", eye[:, :], diff, 0.0, None, ALU.is_equal)
                    return
                link(ve, ve.tensor_tensor(xor, xor, row, ALU.bitwise_xor), "masks")
                ts("masks", upper[:, :], diff, 0.0, None, ALU.is_gt)
                ts("masks", lower[:, :], diff, 0.0, None, ALU.is_lt)
                for k in range(1, LEVELS):
                    stt("masks", level_mask[:, k, :], xor, float(2 ** (k - 1)), upper[:, :], ALU.is_ge, ALU.mult)

            def mixers(n):
                if n == 1:
                    link(ve, ve.memset(half_pi[:, :], TWO_PI / 4), "half_pi")
                    masks(False)
                if n == 11:
                    masks(True)
                if n == 2 or n == 3:
                    s5_decay(n - 2)
                if n == 4:
                    s5_angle()
                if n == 6:
                    s5_input_gain()
                if n == 7 or n == 8:
                    s5_input_weights(n - 7)
                if n == AT["norm1"] + 1:
                    mean("norm1", var[:, :], SEQ)
                    ve.nop().then_inc(S("norm1_var"), 1)
                    token_norm("norm1")
                if n == 10:
                    ve.wait_ge(S("hg_ln"), 1)
                    wait_product(ve, "s5_bT")
                    f = flat(HG_FF)
                    stt("hg_sp", T[2], f, 0.0, T[0], ALU.max, ALU.add)
                    stt("hg_lf", T[1], f, 0.0, T[0], ALU.min, ALU.subtract)
                    link(ve, ve.memset(T[3], 0.0), "hg_ex0")
                for k in range(1, LEVELS + 1):
                    if n == AT[f"lev{k}"]:
                        W = halves(T4[4 + k % 2], 2 ** (k - 1))
                        ve.wait_ge(S("hg_decay"), 2 * k)
                        ve.tensor_tensor(W[1], W[1], halves(HG_QQ, 2 ** (k - 1))[1], ALU.mult).then_inc(S("hg_factors"), 1)
                        ve.tensor_tensor(W[0], W[0], halves(T4[2], 2 ** (k - 1))[0], ALU.mult).then_inc(S("hg_factors"), 1)
                full = [P, 8, P]
                for k in range(LEVELS + 1):
                    if n == AT[f"lev{k}"] + 1:
                        wait_product(ve, f"lev{k}")
                        ps = product(f"lev{k}").rearrange("p (s t) -> p s t", t=P)
                        if k == 0:
                            ins = ve.tensor_tensor(T2[6], ps, bc(eye[:, :].unsqueeze(1), full), ALU.mult)
                        elif k < LEVELS:
                            ins = ve.copy_predicated(T2[6], bc(level_mask[:, k:k + 1, :], full), ps)
                        else:
                            ins = ve.tensor_copy(T[0][:, 0:512], product("lev8")[:, 0:512])
                        taken(ins, f"lev{k}")
                        wait_taken(ve, f"lev{k}")
                if n == AT["hg_ss"] + 1:
                    mean("hg_ss", T[2], 1024)
                    ve.nop().then_inc(S("hg_var"), 1)
                if n == AT["hg_ss"] + 2:
                    inverse_root("hg", T[2], T[3], T[4])
                if n == AT["hg_ss"] + 3:
                    ve.wait_ge(S("hg_sig"), 1)
                    tt("hg_norm", flat(HG_GG), flat(HG_GG), T[5], ALU.mult)
                    tt("hg_norm", flat(HG_II), flat(HG_II), T[3], ALU.mult)
                    for c in range(HEADS):
                        stt("hg_out", HG_GG[:, c, :], HG_II[:, c, :], gain_hg[:, c:c + 1], HG_GG[:, c, :], ALU.mult, ALU.mult)
                if n == AT["q_ss"] + 1:
                    mean("q_ss", T[2], 1024)
                    ve.nop().then_inc(S("q_var"), 1)
                    mean("k_ss", T[5], 1024)
                    ve.nop().then_inc(S("k_var"), 1)
                if n == AT["q_ss"] + 2:
                    inverse_root("q", T[2], T[3], T[4])
                    ts("sb_gain", gain_sb[:, 0:1], gain_sb[:, 0:1], P ** -0.5, None, ALU.mult)
                    stt("q_normed", flat(SQ), flat(SQ), gain_sb[:, 0:1], T[3], ALU.mult, ALU.mult)
                if n == AT["q_ss"] + 3:
                    inverse_root("k", T[5], T[6], T[4])
                    stt("k_normed", flat(SK), flat(SK), gain_sb[:, 1:2], T[6], ALU.mult, ALU.mult)

                def causal(name, x):
                    for hh in range(2):
                        for at, step in ((0, SEQ), (512, P)):
                            v = x[:, 768 * hh + at:768 * hh + at + 2 * step].rearrange("p (i t) -> p i t", i=2)[:, :, 0:P]
                            tt(name, v, v, bc(upper[:, :].unsqueeze(1), [P, 2, P]), ALU.mult)

                if n == AT["z0"] + 2:
                    ve.wait_ge(S("sb_ln"), 1)
                    stt("sb_sp", SOFTP, Z, 0.0, LOG1P, ALU.max, ALU.add)
                    stt("sb_ls", Z, Z, 0.0, LOG1P, ALU.min, ALU.subtract)
                    causal("sb_masked", SOFTP)
                if n == AT["within0"] + 1:
                    for hh in range(2):
                        wait_product(ve, f"within{hh}")
                        z = Z[:, 768 * hh:768 * (hh + 1)]
                        taken(ve.tensor_tensor(z, z, product(f"within{hh}")[:, 0:768], ALU.subtract), f"within{hh}")
                if n == AT["within0"] + 2:
                    ve.wait_ge(S("sb_wexp"), 1)
                    causal("sb_w", Z)
                for g in range(4):
                    if n == TABLE_AT[g] + 2:
                        ve.wait_ge(S("s5_phase"), 3 * (g + 1))
                        cos, sin = s5_tables(g)
                        for i in range(4):
                            s_ = 4 * g + i
                            stt("s5_phase2", cos[:, i, :], time_f[:, :], s5v("turns_lo")[:, s_:s_ + 1], cos[:, i, :], ALU.mult, ALU.add)
                        ts("s5_phase2", flat(sin), flat(cos), MAGIC, MAGIC, ALU.add, ALU.subtract)
                        tt("s5_phase2", flat(cos), flat(cos), flat(sin), ALU.subtract)
                for k in range(8):
                    if n == AT[f"bu{k}"] + 1:
                        wait_product(ve, f"bu{k}")
                        ve.wait_ge(S("s5_table"), 3 * (k // 2 + 1))
                        if k >= 2:
                            ve.wait_ge(S("s5_x"), 2 * (k - 1))
                        cos, sin = (t[:, s5_slice(k), :] for t in s5_tables(k // 2))
                        bu = product(f"bu{k}").rearrange("p (i r t) -> p r i t", i=2, r=2)
                        re, im = bu[:, 0], bu[:, 1]
                        y_re, y_im, t0, t1 = T4[4][:, s5_slice(k), :], T4[5][:, s5_slice(k), :], T4[6][:, 0:2, :], T4[6][:, 2:4, :]
                        tt("s5_rot", y_re, re, cos, ALU.mult)
                        tt("s5_rot", t0, im, sin, ALU.mult)
                        tt("s5_rot", y_im, im, cos, ALU.mult)
                        taken(ve.tensor_tensor(t1, re, sin, ALU.mult), f"bu{k}")
                        wait_taken(ve, f"bu{k}")
                        tt("s5_rot", y_re, y_re, t0, ALU.add)
                        tt("s5_rot", y_im, y_im, t1, ALU.subtract)
                        for y in (y_re, y_im):
                            for i in range(2):
                                v = y[:, i, :]
                                link(ve, ve.tensor_tensor_scan(v, bc(s5v("mag")[:, 2 * k + i:2 * k + i + 1], [P, SEQ]), v,
                                                               0.0, ALU.mult, ALU.add), "s5_scan")
                for c in range(CT):
                    if n == AT[f"s5_y{c}"] + 1:
                        wait_product(ve, f"s5_y{c}")
                        ins = ve.scalar_tensor_tensor(UU[:, c, :], UU[:, c, :], skip_s5[:, c:c + 1], product(f"s5_y{c}")[:, 0:SEQ],
                                                      ALU.mult, ALU.add)
                        taken(ins, f"s5_y{c}")
                        wait_taken(ve, f"s5_y{c}")
                        ve.nop().then_inc(S("s5_y"), 1)
                if n == 74:
                    ve.wait_ge(S("gelu_sq"), 1)
                    ts("gelu_arg", T[4], T[4], 0.044715, 1.0, ALU.mult, ALU.add)
                    tt("gelu_arg", T[4], T[4], flat(UU), ALU.mult)
                if n == 75:
                    ve.wait_ge(S("gelu_sig"), 1)
                    tt("gelu", flat(UU), flat(UU), T[4], ALU.mult)
                if n == 76:
                    ve.wait_ge(S("glu_in_hi"), 1)
                    tt("glu_in_lo", glu_in[:, :, 1, :], UU, glu_in[:, :, 0, :].bitcast(F32), ALU.subtract)
                if n == 78:
                    for m, (o, x) in enumerate(((o_hg, HG_GG), (o_sb, HG_II))):
                        ve.wait_ge(S("o_hi"), m + 1)
                        tt("o_split", o[:, :, 1, :], x, o[:, :, 0, :].bitcast(F32), ALU.subtract)

            for kind, k in HEAD_ORDER:
                if kind == "w":
                    lo(0, RING, k)
                    continue
                for c in range(4 * k, 4 * k + 4):
                    ve.wait_ge(S("a_in_hi"), c + 1)
                    ve.scalar_tensor_tensor(a_in[:, c, 1, :], x_first[:, c, :], gain_mix[:, c:c + 1], a_in[:, c, 0, :].bitcast(F32),
                                            ALU.mult, ALU.subtract).then_inc(S("a_in_lo"), 1)

            for n in range(IN_TILES):
                for p in (2 * n + 4, 2 * n + 5):
                    lo(0, RING, p)
                add_halves(n, n, proj(n))
                mixers(n + 1)

            def glu_split(m):
                ve.wait_ge(S("o_s5_hi"), m + 1)
                ve.tensor_tensor(o_s5[:, m, 1, :], HG_FF[:, m, :], o_s5[:, m, 0, :].bitcast(F32), ALU.subtract)\
                    .then_inc(S("o_s5_lo"), 1)

            for m in range(CT):
                add_halves(GLU_T + 2 * m, 2 * m, HG_FF[:, m, :])
                add_halves(GLU_T + 2 * m + 1, 2 * m + 1, HG_QQ[:, m, :])
                lo(0, RING, BR_P + m, PIECE if m % 2 == 0 else CT)
                ve.wait_ge(S("glu_sig"), m + 1)
                tt("glu_out", HG_FF[:, m, :], HG_FF[:, m, :], HG_QQ[:, m, :], ALU.mult)
                if m:
                    glu_split(m - 1)
            glu_split(CT - 1)

            def merged_lo(u, j):
                ve.wait_ge(S("merged_hi"), u + 1)
                ve.tensor_tensor(a_in[:, u, 1, :], merged[:, j % 2, :], a_in[:, u, 0, :].bitcast(F32), ALU.subtract)\
                    .then_inc(S("merged_lo"), 1)

            def branches(i, last):
                first = isinstance(i, int) and i == 0
                for j in range(RING):
                    for b in range(3):
                        if b:
                            if last and j >= 2:
                                lo(0, RING, OUT_P + 2 * (j - 2) + b - 1)
                            else:
                                lo(i, 2 * RING, BR_P + 2 * (j + 2) + b - 1, PIECE if b == 1 else CT)
                        if not (first and j < 2):
                            ve.wait_ge(S("merged"), i * RING + (j - 1))
                        add_halves(i * (3 * RING) + (BR_T + 3 * j + b), 3 * j + b, gated[:, (3 * j + b) % 6, :])
                    if not (first and j == 0):
                        merged_lo(i * RING + (j - 1), j - 1)

            branches(0, False)
            with ve.Fori(1, KT // RING - 1) as i:
                branches(i, False)
            branches(KT // RING - 1, True)
            merged_lo(KT - 1, KT - 1)

            def outs(i, last):
                for j in range(BANKS):
                    for c in range(2):
                        if last and j >= 2:
                            lo(0, RING, UP_P + 2 * (j - 2) + c)
                        else:
                            lo(i, 2 * BANKS, OUT_P + 2 * (j + 2) + c)
                    t = i * BANKS + j
                    add_halves(i * BANKS + (OUT_T + j), j, convd[:, j, :])
                    ve.wait_ge(tile_summed, i * BANKS + (OUT_T + j + 1))
                    ve.wait_ge(S("x1_landed"), 16)
                    ve.tensor_tensor(x1[:, t, :], x1[:, t, :], convd[:, j, :], ALU.add).then_inc(S("x1_ready"), 1)
                    ve.wait_ge(S("h2_hi"), i * BANKS + (j + 1))
                    ve.scalar_tensor_tensor(h2[:, t, 1, :], x1[:, t, :], gain_ffn[:, bass.ds(t, 1)], h2[:, t, 0, :].bitcast(F32),
                                            ALU.mult, ALU.subtract).then_inc(S("h2_lo"), 1)

            with ve.Fori(0, OUT_TILES // BANKS - 1) as i:
                outs(i, False)
            outs(OUT_TILES // BANKS - 1, True)

            def conv(i, j):
                t = i * BANKS + j
                ve.wait_ge(S("tap2"), t + 1)
                c = convd[:, j % 4, :]
                ve.scalar_tensor_tensor(c, padded[:, j % 2, 1:SEQ + 1], taps[:, t, 1:2], c, ALU.mult, ALU.add).then_inc(S("tap1"), 1)
                ve.wait_ge(S("tap1"), t + 1)
                ve.scalar_tensor_tensor(c, padded[:, j % 2, 0:SEQ], taps[:, t, 0:1], c, ALU.mult, ALU.add).then_inc(S("conv_done"), 1)

            def hidden(q, j):
                ve.wait_ge(S("silu_done"), q + 1)
                c = convd[:, (j - 2) % 4, :]
                ve.tensor_tensor(c, silu[:, :], c, ALU.mult).then_inc(S("hidden"), 1)

            def hidden_lo(q, j):
                ve.wait_ge(S("act_hi"), q + 1)
                ve.tensor_tensor(act[:, q, 1, :], convd[:, (j - 2) % 4, :], act[:, q, 0, :].bitcast(F32), ALU.subtract)\
                    .then_inc(S("act_lo"), 1)

            def ups(i, last):
                first = isinstance(i, int) and i == 0
                for j in range(BANKS):
                    pair_due = j % 2 == 1 and not (first and j < 3)
                    q = i * 2 + (j - 3) // 2
                    for c in range(2):
                        if last and j >= 2:
                            lo(0, RING, DOWN_P + 2 * (j - 2) + c)
                        else:
                            lo(i, 2 * BANKS, UP_P + 2 * (j + 2) + c)
                    if first and j == 1:
                        mean("norm2", var[:, :], SEQ)
                        ve.nop().then_inc(S("norm2_var"), 1)
                        token_norm("norm2")
                    if not (first and j < 2):
                        ve.wait_ge(S("up_scaled"), i * BANKS + (j - 1))
                    add_halves(i * BANKS + (UP_T + j), j, sum_u[:, j % 2, :])
                    if pair_due:
                        hidden(q, j)
                    if not (first and j == 0):
                        conv(i, j - 1)
                    if pair_due:
                        hidden_lo(q, j)

            ups(0, False)
            with ve.Fori(1, UP_TILES // BANKS - 1) as i:
                ups(i, False)
            ups(UP_TILES // BANKS - 1, True)
            conv(UP_TILES // BANKS, -1)
            hidden(FT - 1, 1)
            hidden_lo(FT - 1, 1)

            def downs(i, last):
                n_p = len(DOWN_PIECES)
                for j in range(BANKS):
                    for c in range(n_p):
                        p = j * n_p + RING + c
                        if not last or p < BANKS * n_p:
                            lo(i, BANKS * n_p, DOWN_P + p, DOWN_PIECES[p % n_p])
                    t = i * BANKS + j
                    add_halves(i * BANKS + (DOWN_T + j), j, convd[:, j, :])
                    ve.wait_ge(tile_summed, i * BANKS + (DOWN_T + j + 1))
                    ve.tensor_tensor(x1[:, t, :], x1[:, t, :], convd[:, j, :], ALU.add).then_inc(S("y_ready"), 1)

            with ve.Fori(0, DOWN_TILES // BANKS - 1) as i:
                downs(i, False)
            downs(DOWN_TILES // BANKS - 1, True)

        @block.gpsimd
        def _(pool):
            def tt(name, out_, a, b, op):
                link(pool, pool.tensor_tensor(out_, a, b, op), name)

            b = T[0].rearrange("p (r x) -> p r x", r=4)
            pool.dma_start(s5_in[:, :, :], s5_small).then_inc(S("s5_landed"), 16)
            pool.dma_start(b[:, 0:2, :], s5_b).then_inc(S("s5_landed"), 16)
            link(pool, pool.memset(s5_cT[:, :, :, :, :], 0.0), "s5_zero")
            for r in range(2):
                for g in range(2):
                    pool.dma_start(s5_cT[64 * g:64 * g + 64, r, :, g, :], s5_c[64 * g:64 * g + 64, r, :, :]).then_inc(S("s5_landed"), 16)
            for dst, src in ((gain_ffn, norm_ffn), (gain_hg, hg_gain), (gain_sb, sb_gain), (skip_s5, s5_skip)):
                pool.dma_start(dst[:, :], src).then_inc(S("s5_landed"), 16)
            pool.dma_start(taps[:, :, :], conv).then_inc(S("s5_landed"), 16)
            link(pool, pool.memset(ones[:, :], 1.0), "ones")
            link(pool, pool.memset(T[1], 0.0), "s5_zero")
            ints = T[4].bitcast(I32)
            for c, (step, mult) in enumerate(((1, -1), (1, 0), (0, 1))):
                link(pool, pool.iota(ints[:, c * P:(c + 1) * P], [[step, P]], base=0, channel_multiplier=mult), "iota")
            link(pool, pool.iota(T[5][:, 0:SEQ].bitcast(I32), [[1, SEQ]], base=0, channel_multiplier=0), "time_i")
            link(pool, pool.tensor_copy(time_f[:, :], T[5][:, 0:SEQ].bitcast(I32)), "time_f")

            pool.wait_ge(S("x_sq"), 4)
            for m in (8, 4, 2, 1):
                tt("x_sq_sum", squares[:, 0:m, :], squares[:, 0:m, :], squares[:, m:2 * m, :], ALU.add)

            def scale(n):
                if n == 0:
                    pool.wait_ge(S("norm1_rstd"), 1)
                pool.wait_ge(tile_summed, n + 1)
                pool.tensor_tensor(proj(n), proj(n), rstd[:, :], ALU.mult).then_inc(tile_scaled, 1)

            def mixers(n):
                for k in range(1, LEVELS):
                    if n == AT[f"lev{k}"]:
                        pool.wait_ge(S("hg_decay"), 2 * k)
                        h = 2 ** (k - 1)
                        pre, suf = halves(T4[1], h), halves(T4[3], h)
                        shape = [P, 1024 // (2 * h), h]
                        tt("hg_segments", suf[0], suf[0], bc(pre[1][:, :, h - 1:h], shape), ALU.add)
                        tt("hg_segments", pre[1], pre[1], bc(pre[0][:, :, h - 1:h], shape), ALU.add)
                for g in range(4):
                    if n == TABLE_AT[g]:
                        cos, sin = s5_tables(g)
                        if g == 0:
                            pool.wait_ge(S("sb_ls"), 1)
                        if g == 1:
                            wait_product(pool, "sb_o")
                        tt("s5_phase", cos, bc(time_f[:, :].unsqueeze(1), [P, 4, SEQ]),
                           bc(s5v("turns")[:, 4 * g:4 * g + 4].unsqueeze(2), [P, 4, SEQ]), ALU.mult)
                        link(pool, pool.tensor_scalar(flat(sin), flat(cos), MAGIC, MAGIC, ALU.add, ALU.subtract), "s5_phase")
                        tt("s5_phase", flat(cos), flat(cos), flat(sin), ALU.subtract)
                for k in range(8):
                    if n == AT[f"bu{k}"] + 2:
                        pool.wait_ge(S("s5_scan"), 4 * (k + 1))
                        c = k // 2
                        if k % 2 == 0 and c > 0:
                            wait_product(pool, f"s5_y{c - 1}")
                        cos, sin = (t[:, s5_slice(k), :].rearrange("p a b -> p (a b)") for t in s5_tables(c))
                        h = slice(512 * (k % 2), 512 * (k % 2) + 512)
                        y_re, y_im = T[4][:, h], T[5][:, h]
                        t0, t1 = (proj1[:, 2, 2 * i:2 * i + 2, :].rearrange("p a b -> p (a b)") for i in range(2))
                        x = [proj1[:, r, s5_slice(k), :].rearrange("p a b -> p (a b)") for r in range(2)]
                        tt("s5_unrot", t0, y_re, cos, ALU.mult)
                        tt("s5_unrot", t1, y_im, sin, ALU.mult)
                        tt("s5_x", x[0], t0, t1, ALU.subtract)
                        tt("s5_unrot", t0, y_re, sin, ALU.mult)
                        tt("s5_unrot", t1, y_im, cos, ALU.mult)
                        tt("s5_x", x[1], t0, t1, ALU.add)

            for n in range(IN_TILES):
                scale(n)
                mixers(n + 1)

            pool.wait_ge(S("o_split"), 2)
            pool.wait_ge(S("o_s5_lo"), CT)
            pool.dma_start(x1[:, :, :], xT).then_inc(S("x1_landed"), 16)

            pool.wait_ge(S("gate_ready"), 12)

            def merge(i):
                for j in range(RING):
                    u = i * RING + j
                    for b in range(3):
                        g = gated[:, (3 * j + b) % 6, :]
                        pool.wait_ge(tile_summed, i * (3 * RING) + (BR_T + 3 * j + b + 1))
                        pool.tensor_tensor(g, g, gates[:, i * (3 * RING) + (3 * j + b), :], ALU.mult).then_inc(S("gated"), 1)
                    if not (isinstance(i, int) and i == 0 and j < 2):
                        pool.wait_ge(S("merged_lo"), i * RING + (j - 1))
                    m = merged[:, j % 2, :]
                    pool.wait_ge(S("gated"), i * (3 * RING) + (3 * j + 3))
                    pool.tensor_tensor(m, gated[:, (3 * j) % 6, :], gated[:, (3 * j + 1) % 6, :], ALU.add).then_inc(S("merged2"), 1)
                    pool.wait_ge(S("merged2"), u + 1)
                    pool.tensor_tensor(m, m, gated[:, (3 * j + 2) % 6, :], ALU.add).then_inc(S("merged"), 1)

            merge(0)
            with pool.Fori(1, KT // RING) as i:
                merge(i)

            pool.wait_ge(S("x1_ready"), 1)
            link(pool, pool.tensor_tensor(root[:, :], x1[:, 0, :], x1[:, 0, :], ALU.mult), "x1_sq_sum")
            with pool.Fori(1, KT) as i:
                pool.wait_ge(S("x1_ready"), i + 1)
                pool.tensor_tensor(silu[:, :], x1[:, i, :], x1[:, i, :], ALU.mult).then_inc(S("x1_sq"), 1)
                pool.wait_ge(S("x1_sq"), i)
                pool.tensor_tensor(root[:, :], root[:, :], silu[:, :], ALU.add).then_inc(S("x1_sq_sum"), 1)
                pool.wait_ge(S("x1_sq_sum"), i + 1)

            link(pool, pool.memset(padded[:, :, 0:2], 0.0), "pad_zero")
            pool.wait_ge(S("norm2_rstd"), 1)

            def up_scale(i):
                for j in range(2):
                    t = i * 2 + j
                    pool.wait_ge(tile_summed, i * 2 + (UP_T + j + 1))
                    if not isinstance(i, int):
                        pool.wait_ge(S("conv_done"), t - 1)
                    pool.tensor_tensor(padded[:, j, 2:], sum_u[:, j, :], rstd[:, :], ALU.mult).then_inc(S("up_scaled"), 1)

            up_scale(0)
            with pool.Fori(1, UP_TILES // 2) as i:
                up_scale(i)

            with pool.Fori(0, DOWN_TILES // BANKS - 1) as i:
                pool.wait_ge(S("y_ready"), i * BANKS + BANKS)
                pool.dma_start(out[i, :, :, :], x1[:, bass.ds(i * BANKS, BANKS), :]).then_inc(S("stored"), 16)
            pool.wait_ge(S("stored"), 16 * (DOWN_TILES // BANKS - 1))


def kernel(**inputs):
    import numpy as np
    import concourse.bacc as bacc
    from concourse.bass_utils import run_bass_kernel_spmd

    a = {k: np.asarray(v) for k, v in inputs.items()}
    width = PIECE * P

    def tiles(w, cols):
        return w.reshape(-1, P, w.shape[1] // P, P).transpose(2, 1, 0, 3)[cols]

    def pieces(w, cols):
        t = tiles(w, cols)
        return np.ascontiguousarray(t.reshape(len(cols), P, 2, width).transpose(0, 2, 1, 3).reshape(-1, P, width))

    def columns(v):
        return np.ascontiguousarray(v.reshape(-1, P).T)

    order = [1, 0, 2, 3, 4, 5, 6, 7]
    in_cols = [CT * g + c for g in order for c in range(CT)]
    in_cols += [8 * CT + KT * b + j for j in range(KT) for b in (0, 2, 1)]
    up_cols = [h * FT + t for t in range(FT) for h in range(2)]
    glu = tiles(a["s5_w_glu"][0], [h * CT + c for c in range(CT) for h in range(2)])
    w_branch = np.stack([tiles(a["w_branch"][0, b], list(range(KT))) for b in (0, 2, 1)], 2)

    def states(v):
        v = v.reshape((ST, P) + v.shape[2:])
        return v.transpose((1, 0) + tuple(range(2, v.ndim)))

    arrays = {
        "xT": a["x"][0].reshape(SEQ, KT, P).transpose(2, 1, 0),
        "w_in": pieces(a["w_in"][0], in_cols),
        "w_glu": glu.reshape(CT, 2, P, CT * P).transpose(0, 2, 1, 3).reshape(CT, P, width),
        "w_br": w_branch.reshape(KT, P, N_BRANCH * CT * P),
        "w_out": pieces(a["w_out"][0], list(range(KT))),
        "w_up": pieces(a["w_up"][0], up_cols),
        "w_down": tiles(a["w_down"][0], list(range(KT))).reshape(KT, P, FT * P),
        "norm_mix": columns(a["norm_mix_g"][0]),
        "norm_ffn": columns(a["norm_ffn_g"][0]),
        "hg_gain": columns(a["hg_norm_g"][0]),
        "s5_small": np.stack([states(a["s5_a_re"][0]), states(a["s5_a_im"][0]),
                              states(np.broadcast_to(a["s5_log_dt"][0][:, None], (S5_GROUPS, S5_STATE)))], 1),
        "s5_b": np.stack([states(a[k][0]).reshape(P, ST * S5_CH) for k in ("s5_b_re", "s5_b_im")], 1),
        "s5_c": np.stack([states(a[k][0].transpose(0, 2, 1)) for k in ("s5_c_re", "s5_c_im")], 1),
        "s5_skip": columns(a["s5_d"][0]),
        "sb_gain": np.stack([a["sb_q_g"][0], a["sb_k_g"][0]], 1),
        "conv": a["conv_w"][0].reshape(3, 2, FT, P).transpose(3, 2, 1, 0).reshape(P, UP_TILES, 3),
    }
    nc = bacc.Bacc("TRN2", target_bir_lowering=False, num_devices=1)
    args = []
    for name, v in arrays.items():
        arrays[name] = v = np.ascontiguousarray(v)
        args.append(nc.dram_tensor(name, v.shape, mybir.dt.from_np(v.dtype), kind="ExternalInput").ap())
    args.append(nc.dram_tensor("out", (KT // BANKS, P, BANKS, SEQ), F32, kind="ExternalOutput").ap())
    layer(nc, **dict(zip(list(arrays) + ["out"], args)))
    r = run_bass_kernel_spmd(nc, [arrays], core_ids=[0])
    got = r.results[0]["out"]
    return np.ascontiguousarray(got.transpose(3, 0, 2, 1).reshape(1, SEQ, D_MODEL))
```
